# Optimizing a Trainium2 kernel written in Bass

```python
import math
import jax, jax.numpy as jnp
from jax import lax
import numpy as np

D_MODEL = 1024
BATCH = 1
SEQ = 512
DEPTH = 2
DEC_BATCH = 1
DEC_SEQ = 256
PAST_LEN = 128

RMS_EPS = 1e-6
HEAD_DIM = 64
NEG_INF = -1e30
A_PATTERNS = ((128, 1), (512, 4), (2048, 16))
A_GROUPS = 3
A_HEADS_PER_GROUP = 4
A_HEADS = A_GROUPS * A_HEADS_PER_GROUP
A_BLOCK = 64
A_IN = 3 * A_HEADS * HEAD_DIM
A_OUT = A_HEADS_PER_GROUP * HEAD_DIM
T5_BUCKETS = 32
T5_MAX_DISTANCE = 1024
B_HEADS = 12
B_Q_RANK = 384
B_KV_RANK = 256
B_NOPE = 64
B_ROPE = 32
B_V = 64
B_IN = B_Q_RANK + B_KV_RANK + B_ROPE
B_OUT = B_HEADS * B_V
B_QBLOCK = 128
ROPE_THETA = 10000.0
EVEN_IN = A_IN + B_IN
EVEN_OUT = A_OUT + B_OUT
GRID_W = 64
C_HEADS = 16
C_WIN_ROWS = 8
C_WIN_COLS = 16
C_COL_BLOCK = 16
C_KEY_COLS = C_COL_BLOCK + C_WIN_COLS
C_IN = 3 * C_HEADS * HEAD_DIM
C_OUT = C_HEADS * HEAD_DIM
N_EXPERTS = 16
EXPERT_FF = 1024
CAPACITY_FACTOR = 2
N_EVEN = (DEPTH + 1) // 2
N_ODD = DEPTH // 2

kernel_name = "hybrid_dilated_mla_natten_ec_moe_encoder"

def rms_norm(x, g):
    xf = x.astype(jnp.float32)
    y = xf * lax.rsqrt(jnp.mean(xf * xf, axis=-1, keepdims=True) + RMS_EPS)
    return (y * g.astype(jnp.float32)).astype(x.dtype)

def t5_bucket(rel):
    half = T5_BUCKETS // 2
    max_exact = half // 2
    n = np.abs(rel)
    large = max_exact + (np.log(np.maximum(n, 1) / max_exact) / np.log(T5_MAX_DISTANCE / max_exact) * (half - max_exact)).astype(np.int32)
    large = np.minimum(large, half - 1)
    return (np.where(rel > 0, half, 0) + np.where(n < max_exact, n, large)).astype(np.int32)

def dilated_group_attention(q, k, v, bias_table, window, dilation):
    Bn, S, H, dh = q.shape
    radius = window // (2 * dilation)
    L = S // dilation
    nb = -(-L // A_BLOCK)
    Lp = nb * A_BLOCK

    def to_blocks(t):
        t = t.reshape(Bn, L, dilation, H, dh).transpose(0, 2, 1, 3, 4)
        t = jnp.pad(t, ((0, 0), (0, 0), (0, Lp - L), (0, 0), (0, 0)))
        return t.reshape(Bn, dilation, nb, A_BLOCK, H, dh)

    def band(t):
        tp = jnp.pad(t, ((0, 0), (0, 0), (1, 1), (0, 0), (0, 0), (0, 0)))
        return jnp.concatenate([tp[:, :, :-2], tp[:, :, 1:-1], tp[:, :, 2:]], axis=3)

    qb = to_blocks(q)
    kband = band(to_blocks(k))
    vband = band(to_blocks(v))
    qi = np.arange(A_BLOCK)[:, None]
    ci = np.arange(3 * A_BLOCK)[None, :]
    off = ci - A_BLOCK - qi
    key_m = np.arange(nb)[:, None, None] * A_BLOCK + ci[None] - A_BLOCK
    valid = (np.abs(off) <= radius)[None] & (key_m >= 0) & (key_m < L)
    bias = jnp.transpose(bias_table[t5_bucket(off * dilation)], (2, 0, 1)).astype(jnp.float32)
    s = jnp.einsum('brnqhd,brnkhd->brnhqk', qb, kband).astype(jnp.float32) * (dh ** -0.5)
    s = jnp.where(valid[None, None, :, None], s + bias[None, None, None], NEG_INF)
    m = jnp.max(s, axis=-1, keepdims=True)
    p = jnp.exp(s - m)
    den = jnp.sum(p, axis=-1, keepdims=True)
    o = jnp.einsum('brnhqk,brnkhd->brnqhd', (p / den).astype(v.dtype), vband)
    lse = (m + jnp.log(den))[..., 0]
    o = o.reshape(Bn, dilation, Lp, H, dh)[:, :, :L].transpose(0, 2, 1, 3, 4).reshape(Bn, S, H, dh)
    lse = lse.transpose(0, 1, 2, 4, 3).reshape(Bn, dilation, Lp, H)[:, :, :L].transpose(0, 2, 1, 3).reshape(Bn, S, H)
    return o, lse

def mixer_a(u, t5_table):
    Bn, S, _ = u.shape
    u = u.reshape(Bn, S, 3, A_GROUPS, A_HEADS_PER_GROUP, HEAD_DIM)
    outs, lses = [], []
    for g, (window, dilation) in enumerate(A_PATTERNS):
        tab = t5_table[:, g * A_HEADS_PER_GROUP:(g + 1) * A_HEADS_PER_GROUP]
        o, l = dilated_group_attention(u[:, :, 0, g], u[:, :, 1, g], u[:, :, 2, g], tab, window, dilation)
        outs.append(o)
        lses.append(l)
    wts = jax.nn.softmax(jnp.stack(lses), axis=0)
    o = jnp.einsum('gbsh,gbshd->bshd', wts, jnp.stack(outs).astype(jnp.float32))
    return o.reshape(Bn, S, A_OUT).astype(u.dtype)

def rope_tables(S):
    inv = 1.0 / (ROPE_THETA ** (np.arange(0, B_ROPE, 2, dtype=np.float32) / B_ROPE))
    ang = np.arange(S, dtype=np.float32)[:, None] * inv[None]
    return jnp.asarray(np.cos(ang), dtype=jnp.float32), jnp.asarray(np.sin(ang), dtype=jnp.float32)

def apply_rope(x, cos, sin):
    xf = x.astype(jnp.float32)
    x1, x2 = jnp.split(xf, 2, axis=-1)
    return jnp.concatenate([x1 * cos - x2 * sin, x2 * cos + x1 * sin], axis=-1).astype(x.dtype)

def mixer_b(u, g_qa, w_qb, g_kva, w_kvb):
    Bn, S, _ = u.shape
    c_q, c_kv, k_r = jnp.split(u, [B_Q_RANK, B_Q_RANK + B_KV_RANK], axis=-1)
    q = (rms_norm(c_q, g_qa) @ w_qb).reshape(Bn, S, B_HEADS, B_NOPE + B_ROPE)
    kv = (rms_norm(c_kv, g_kva) @ w_kvb).reshape(Bn, S, B_HEADS, B_NOPE + B_V)
    q_nope, q_rope = q[..., :B_NOPE], q[..., B_NOPE:]
    k_nope, v = kv[..., :B_NOPE], kv[..., B_NOPE:]
    cos, sin = rope_tables(S)
    q_rope = apply_rope(q_rope, cos[:, None, :], sin[:, None, :])
    k_rope = apply_rope(k_r, cos, sin)
    scale = (B_NOPE + B_ROPE) ** -0.5
    nq = S // B_QBLOCK

    def to_qblocks(t):
        return t.reshape(Bn, nq, B_QBLOCK, *t.shape[2:]).swapaxes(0, 1)

    def attend(args):
        qn, qr = args
        s = (jnp.einsum('bqhd,bkhd->bhqk', qn, k_nope).astype(jnp.float32)
             + jnp.einsum('bqhr,bkr->bhqk', qr, k_rope).astype(jnp.float32)) * scale
        p = jax.nn.softmax(s, axis=-1).astype(v.dtype)
        return jnp.einsum('bhqk,bkhd->bqhd', p, v)

    o = lax.map(attend, (to_qblocks(q_nope), to_qblocks(q_rope)))
    return o.swapaxes(0, 1).reshape(Bn, S, B_OUT)

def mixer_c(u, rpb):
    Bn, S, _ = u.shape
    rows = S // GRID_W
    wr = min(C_WIN_ROWS, rows)
    u = u.reshape(Bn, rows, GRID_W, 3, C_HEADS, HEAD_DIM)
    q, k, v = u[:, :, :, 0], u[:, :, :, 1], u[:, :, :, 2]
    n_cb = GRID_W // C_COL_BLOCK
    qcol = np.arange(GRID_W).reshape(n_cb, C_COL_BLOCK)
    kstart = np.clip(np.arange(n_cb) * C_COL_BLOCK - C_WIN_COLS // 2, 0, GRID_W - C_KEY_COLS)
    kcol = kstart[:, None] + np.arange(C_KEY_COLS)[None]
    wstart = np.clip(qcol - C_WIN_COLS // 2, 0, GRID_W - C_WIN_COLS)
    col_valid = (kcol[:, None, :] >= wstart[..., None]) & (kcol[:, None, :] < wstart[..., None] + C_WIN_COLS)
    dcol_idx = np.clip(kcol[:, None, :] - qcol[..., None] + C_WIN_COLS - 1, 0, 2 * C_WIN_COLS - 2)
    rpb_cols = rpb.astype(jnp.float32)[:, :, dcol_idx]
    k_cols = k[:, :, kcol]
    v_cols = v[:, :, kcol]
    mask = col_valid[None, None, :, :, None, :]
    scale = HEAD_DIM ** -0.5

    def attend_row(r):
        r0 = jnp.clip(r - wr // 2, 0, rows - wr)
        kr = lax.dynamic_slice_in_dim(k_cols, r0, wr, axis=1)
        vr = lax.dynamic_slice_in_dim(v_cols, r0, wr, axis=1)
        qr = lax.dynamic_index_in_dim(q, r, axis=1, keepdims=False).reshape(Bn, n_cb, C_COL_BLOCK, C_HEADS, HEAD_DIM)
        s = jnp.einsum('bjqhd,bwjchd->bhjqwc', qr, kr).astype(jnp.float32) * scale
        drow = r0 + jnp.arange(wr) - r + C_WIN_ROWS - 1
        bias = jnp.take(rpb_cols, drow, axis=1).transpose(0, 2, 3, 1, 4)
        s = jnp.where(mask, s + bias[None], NEG_INF)
        shp = s.shape
        p = jax.nn.softmax(s.reshape(Bn, C_HEADS, n_cb, C_COL_BLOCK, wr * C_KEY_COLS), axis=-1).reshape(shp)
        o = jnp.einsum('bhjqwc,bwjchd->bjqhd', p.astype(v.dtype), vr)
        return o.reshape(Bn, GRID_W, C_OUT)

    o = lax.map(attend_row, jnp.arange(rows))
    return o.transpose(1, 0, 2, 3).reshape(Bn, S, C_OUT)

def expert_choice_ffn(h, router, w_gate, w_up, w_down):
    Bn, S, D = h.shape
    T = Bn * S
    cap = CAPACITY_FACTOR * T // N_EXPERTS
    xt = h.reshape(T, D)
    aff = jax.nn.softmax((xt @ router).astype(jnp.float32), axis=-1)
    gate, idx = lax.top_k(aff.T, cap)
    xe = xt[idx]
    hid = jax.nn.silu(jnp.einsum('ecd,edf->ecf', xe, w_gate)) * jnp.einsum('ecd,edf->ecf', xe, w_up)
    ye = jnp.einsum('ecf,efd->ecd', hid, w_down) * gate[..., None].astype(h.dtype)
    out = jnp.zeros_like(xt).at[idx.reshape(-1)].add(ye.reshape(-1, D))
    return out.reshape(Bn, S, D)

def trunk(x, ln_mix_g, w_in_even, g_qa, w_qb, g_kva, w_kvb, t5_table, w_out_even,
          w_in_odd, rpb, w_out_odd, ln_ffn_g, router, w_gate, w_up, w_down, final_g):
    for layer in range(DEPTH):
        i = layer // 2
        h = rms_norm(x, ln_mix_g[layer])
        if layer % 2 == 0:
            u = h @ w_in_even[i]
            a = mixer_a(u[..., :A_IN], t5_table)
            b = mixer_b(u[..., A_IN:], g_qa[i], w_qb[i], g_kva[i], w_kvb[i])
            mix = jnp.concatenate([a, b], axis=-1) @ w_out_even[i]
        else:
            mix = mixer_c(h @ w_in_odd[i], rpb[i]) @ w_out_odd[i]
        x = x + mix
        x = x + expert_choice_ffn(rms_norm(x, ln_ffn_g[layer]), router[layer], w_gate[layer], w_up[layer], w_down[layer])
    return rms_norm(x, final_g)

def setup_inputs(seed: int = 0) -> dict:
    key = jax.random.key(seed)
    ks = jax.random.split(key, 24)

    def nrm(k, shape, scale):
        return jax.random.normal(k, shape, jnp.float32) * scale

    def gain(k, shape):
        return 1.0 + 0.02 * jax.random.normal(k, shape, jnp.float32)

    return {
        "x_prompt": jax.random.normal(ks[0], (BATCH, SEQ, D_MODEL), jnp.float32),
        "x_sample": jax.random.normal(ks[1], (DEC_BATCH, DEC_SEQ, D_MODEL), jnp.float32),
        "ln_mix_g": gain(ks[2], (DEPTH, D_MODEL)),
        "w_in_even": nrm(ks[3], (N_EVEN, D_MODEL, EVEN_IN), D_MODEL ** -0.5),
        "g_qa": gain(ks[4], (N_EVEN, B_Q_RANK)),
        "w_qb": nrm(ks[5], (N_EVEN, B_Q_RANK, B_HEADS * (B_NOPE + B_ROPE)), B_Q_RANK ** -0.5),
        "g_kva": gain(ks[6], (N_EVEN, B_KV_RANK)),
        "w_kvb": nrm(ks[7], (N_EVEN, B_KV_RANK, B_HEADS * (B_NOPE + B_V)), B_KV_RANK ** -0.5),
        "t5_table": nrm(ks[8], (T5_BUCKETS, A_HEADS), 0.2),
        "w_out_even": nrm(ks[9], (N_EVEN, EVEN_OUT, D_MODEL), EVEN_OUT ** -0.5),
        "w_in_odd": nrm(ks[10], (N_ODD, D_MODEL, C_IN), D_MODEL ** -0.5),
        "rpb": nrm(ks[11], (N_ODD, C_HEADS, 2 * C_WIN_ROWS - 1, 2 * C_WIN_COLS - 1), 0.2),
        "w_out_odd": nrm(ks[12], (N_ODD, C_OUT, D_MODEL), C_OUT ** -0.5),
        "ln_ffn_g": gain(ks[13], (DEPTH, D_MODEL)),
        "router": nrm(ks[14], (DEPTH, D_MODEL, N_EXPERTS), D_MODEL ** -0.5),
        "w_gate": nrm(ks[15], (DEPTH, N_EXPERTS, D_MODEL, EXPERT_FF), D_MODEL ** -0.5),
        "w_up": nrm(ks[16], (DEPTH, N_EXPERTS, D_MODEL, EXPERT_FF), D_MODEL ** -0.5),
        "w_down": nrm(ks[17], (DEPTH, N_EXPERTS, EXPERT_FF, D_MODEL), EXPERT_FF ** -0.5),
        "final_g": gain(ks[18], (D_MODEL,)),
    }

def reference(x_prompt, x_sample, ln_mix_g, w_in_even, g_qa, w_qb, g_kva, w_kvb, t5_table, w_out_even,
              w_in_odd, rpb, w_out_odd, ln_ffn_g, router, w_gate, w_up, w_down, final_g):
    y_prompt = trunk(x_prompt, ln_mix_g, w_in_even, g_qa, w_qb, g_kva, w_kvb, t5_table, w_out_even,
                     w_in_odd, rpb, w_out_odd, ln_ffn_g, router, w_gate, w_up, w_down, final_g)
    y_sample = trunk(x_sample, ln_mix_g, w_in_even, g_qa, w_qb, g_kva, w_kvb, t5_table, w_out_even,
                     w_in_odd, rpb, w_out_odd, ln_ffn_g, router, w_gate, w_up, w_down, final_g)
    return (y_prompt, y_sample)


_drawn_inputs = setup_inputs


def setup_inputs(seed=0):
    import zlib

    import numpy as np

    out = dict(_drawn_inputs(seed))
    spreads = {}
    factors = {'ln_mix_g': 3.587,
     'g_qa': 7.273,
     'g_kva': 5.216,
     't5_table': 2.775,
     'final_g': 8.403,
     'ln_ffn_g': 5.22}
    for name, (base, spread) in spreads.items():
        noise = np.random.default_rng([zlib.crc32(name.encode()), seed]).standard_normal(out[name].shape)
        drawn = base * np.exp(spread * noise) if base else spread * noise
        out[name] = __import__('jax').numpy.asarray(drawn.astype(out[name].dtype))
    for name, factor in factors.items():
        out[name] = (out[name] * factor).astype(out[name].dtype)
    return out
```

```python
from contextlib import ExitStack

import concourse.bass as bass
from concourse import mybir

F32 = mybir.dt.float32
U32 = mybir.dt.uint32
ALU = mybir.AluOpType
ACT = mybir.ActivationFunctionType
AX = mybir.AxisListType

P = 128
D = 1024
DC = D // P
PROMPT, SAMPLE = 512, 256
TOK = PROMPT + SAMPLE
NT = TOK // P
HALF = TOK // 2
HD = 64
EPS = 1e-6
MASKED = -1e30
GROUPS = 3
AH = 4
A_IN = 3 * GROUPS * AH * HD
QR, KVR, ROPE = 384, 256, 32
B_IN = QR + KVR + ROPE
B_PAIRS = 6
C_PAIRS = 8
GRID = 64
CB = 16
NB = GRID // CB
C_ROWS, S_ROWS = PROMPT // GRID, SAMPLE // GRID
WIN = 3 * CB
DROWS = 15
NE = 16
FF = 1024
CAP_P, CAP_S = 2 * PROMPT // NE, 2 * SAMPLE // NE
CAP = CAP_P + CAP_S
OROW = AH * (HD + 2)
LOW = -3.0e38


def after(n):
    return n + 3


class Unit:

    def __init__(self, nq, heads, kt, tiles, first_key, tile, last):
        self.nq, self.heads, self.kt, self.tiles = nq, heads, kt, tiles
        self.nk = kt * len(tiles)
        self.first_key = first_key
        self.tile = tile
        self.last = last

    def cols(self, h):
        return slice(h * self.nk, (h + 1) * self.nk)


def near_tiles(t, n):
    return list(range(max(t - 1, 0), min(t + 2, n)))


def units_near(nq, heads_pairs, t, tile, n, base):
    near = near_tiles(t, n)
    groups = [[h, h + 1] for h in heads_pairs] if len(near) < 3 else [[h + d] for h in heads_pairs for d in (0, 1)]
    return [Unit(nq, g, nq, [base + m for m in near], t, tile, g is groups[-1]) for g in groups]


def units_a(g):
    if g == 0:
        us = [u for t in range(4) for u in units_near(P, (0, 2), t, t, 4, 0)]
        return us + [u for t in range(2) for u in units_near(P, (0, 2), t, 4 + t, 2, 4)]
    us = [Unit(P, [0, 1, 2, 3], P, [t], t, t, True) for t in range(4)]
    return us + [Unit(HD, [0, 1, 2, 3], HD, [4 + t], t, 4 + t, True) for t in range(4)]


def units_b():
    us = [Unit(P, [h], P, [0, 1, 2, 3], 0, t, h == 1) for t in range(4) for h in (0, 1)]
    return us + [Unit(P, [0, 1], P, [4, 5], 0, t, True) for t in (4, 5)]


def units_c():
    us = [u for j in range(NB) for u in units_near(P, (0,), j, j, NB, 0)]
    return us + [u for j in range(NB) for u in units_near_sample(j)]


def units_near_sample(j):
    near = near_tiles(j, NB)
    return [Unit(CB * S_ROWS, [0, 1], CB * S_ROWS, [NB + m for m in near], j, NB + j, True)]


C_BIAS0 = [0, 2, 2, 5]


def tokens_a(ap, g, t):
    if g == 0:
        return ap[:, t * P:(t + 1) * P]
    part = ap[:, 0:PROMPT] if t < 4 else ap[:, PROMPT:TOK]
    t %= 4
    return part.rearrange("p (l r) -> p l r", r=4)[:, :, t]


def tokens_c(ap, t):
    part = ap[:, 0:PROMPT] if t < NB else ap[:, PROMPT:TOK]
    t %= NB
    return part.rearrange("p (r w) -> p r w", w=GRID)[:, :, t * CB:(t + 1) * CB]


def run_c(ap, t, n=1):
    if t < NB:
        return ap[:, t * P:(t + n) * P]
    w = CB * S_ROWS
    return ap[:, PROMPT + (t - NB) * w:PROMPT + (t - NB + n) * w]


def program(nc, x_in, gains, w_a, w_b, w_qb, w_kvb, w_out, w_c, t5, onehot, rpb, router, w_gate, w_up, w_down,
            final_g, ident_in, col_mask, q_table, rope_in, y_out):
    es = ExitStack()
    with es:
        def sb(name, shape, dt=F32):
            return es.enter_context(nc.sbuf_tensor(name, shape, dt))

        def ps(name, shape):
            return es.enter_context(nc.psum_tensor(name, shape, F32))

        def sem(name):
            return es.enter_context(nc.semaphore(name))

        def dram(name, shape):
            return nc.dram_tensor(name, shape, F32, kind="Internal").ap()

        f_dram = dram("t5_by_distance", (12, 1024))
        shifted_dram = dram("t5_shifted", (CB, 12, 1024 - CB))
        window_dram = dram("rpb_windows", (CB, 2 * C_PAIRS, DROWS, WIN))
        oa_dram = dram("mixer_a_groups", (GROUPS, TOK, OROW))
        xn_dram = [dram(f"normed_rows{l}", (TOK, D)) for l in range(2)]
        acc_dram = [dram(f"residual_rows{l}", (TOK, D)) for l in range(2)]

        x = sb("x", [P, NT, D])
        hT = sb("hT", [P, DC, TOK])
        aT = sb("aT", [P, DC, TOK])
        ident = sb("ident", [P, P])
        gcol = sb("gcol", [P, 37])
        g_of = {"mix0": gcol[:, 0:8], "ffn0": gcol[:, 8:16], "mix1": gcol[:, 16:24], "ffn1": gcol[:, 24:32]}
        gq, gkv = gcol[:, 32:35], gcol[:, 35:37]
        router_sb = sb("router_sb", [P, 2, DC, NE])
        smax = sb("smax", [P, 16, AH])
        nmax = sb("nmax", [P, 16, AH])
        den = sb("den", [P, 16, AH])
        rden = sb("rden", [P, 16, AH])
        stat = sb("stat", [P, 5, NT])
        rstd = sb("rstd", [P, 5, NT])
        bstat = sb("bstat", [P, 2, NT])
        brstd = sb("brstd", [P, 2, NT])
        ARENA = 32800
        arena = sb("arena", [P, ARENA])

        class Carve:

            def __init__(self, at=0):
                self.at = at

            def __call__(self, *shape):
                n = 1
                for s in shape:
                    n *= s
                a = arena[:, self.at:self.at + n]
                self.at += n
                assert self.at <= ARENA, self.at
                if len(shape) == 1:
                    return a
                names = " ".join(f"d{i}" for i in range(len(shape)))
                return a.rearrange(f"p ({names}) -> p {names}", **{f"d{i}": s for i, s in enumerate(shape)})

        proj_ps = ps("proj_ps", [P, 2, 512])
        score_ps = ps("score_ps", [P, 2, 512])
        pT_ps = ps("pT_ps", [P, 2, 512])
        o_ps = ps("o_ps", [P, 2, 512])

        seeded = []

        def slots(name):
            s = sem(name)
            seeded.append(s)
            return s

        phases = ["mix0", "a", "join", "b", "out0", "ffn0", "route0", "moe0", "mix1", "c", "out1", "ffn1", "route1", "moe1", "final"]
        ended = sem("ended")

        def end_phase(eng, name):
            eng.drain().then_inc(ended, 1)
            eng.wait_ge(ended, 5 * (phases.index(name) + 1))

        settled = sem("settled")

        def settle(eng):
            eng.sem_inc(settled, 1)

        consts_in = sem("consts_in")

        class Norm:
            def __init__(self, name, k):
                self.name, self.k = name, k
                c = Carve()
                self.xn = c(NT, D)
                self.junk = c(D)
                self.reloads = ("mix0", "mix1", "final").index(name) + 1 if name in ("mix0", "mix1", "final") else 0
                self.t0, self.n0 = NT * k, 2 * NT * k

            def act(self, act):
                if self.reloads:
                    act.wait_ge(x_loaded, 16 * self.reloads)
                for t in range(NT):
                    if t:
                        act.wait_ge(norm_squares, self.t0 + t)
                    act.activation(self.junk, x[:, t], ACT.Square, accum_out=stat[:, self.k, t:t + 1]).then_inc(norm_squares, 1)
                act.wait_ge(norm_mean, self.k + 1)
                act.activation(rstd[:, self.k], rstd[:, self.k], ACT.Sqrt).then_inc(norm_root, 1)
                act.wait_ge(norm_rstd, self.k + 1)
                for t in range(NT):
                    act.activation(self.xn[:, t], x[:, t], ACT.Copy, scale=rstd[:, self.k, t:t + 1]).then_inc(norm_scaled, 1)

            def dve_stats(self, dve):
                dve.wait_ge(norm_squares, self.t0 + NT)
                dve.tensor_scalar(rstd[:, self.k], stat[:, self.k], 1.0 / D, EPS, ALU.mult, ALU.add).then_inc(norm_mean, 1)
                dve.wait_ge(norm_root, self.k + 1)
                dve.reciprocal(rstd[:, self.k], rstd[:, self.k]).then_inc(norm_rstd, 1)

            def pe(self, pe):
                pe.wait_ge(consts_in, CONSTS)
                for t in range(NT):
                    pe.wait_ge(norm_scaled, self.t0 + t + 1)
                    for half in range(2):
                        n = self.n0 + 2 * t + half
                        pe.wait_ge(norm_evac, after(n - 2))
                        for c in range(4):
                            k = 4 * half + c
                            last = pe.transpose(proj_ps[:, half, c * P:(c + 1) * P], self.xn[:, t, k * P:(k + 1) * P], ident[:])
                        last.then_inc(norm_turned, 1)

            def dve(self, dve):
                self.dve_stats(dve)
                g = g_of[self.name]
                dve.wait_ge(consts_in, CONSTS)
                for n in range(2 * NT):
                    t, half = n // 2, n % 2
                    dve.wait_ge(norm_turned, after(self.n0 + n))
                    gg = g[:, 4 * half:4 * half + 4]
                    src = proj_ps[:, half].rearrange("p (c t) -> p c t", c=4)
                    if self.name != "mix1":
                        dve.tensor_tensor(hT[:, 4 * half:4 * half + 4, t * P:(t + 1) * P], src,
                                          gg.unsqueeze(2).to_broadcast([P, 4, P]), ALU.mult).then_inc(norm_evac, 1)
                        continue
                    base, rows, row0 = (0, C_ROWS, 2 * t) if t < 4 else (PROMPT, S_ROWS, 2 * (t - 4))
                    for r in range(P // GRID):
                        for b in range(NB):
                            at = base + (b * rows + row0 + r) * CB
                            last = dve.tensor_tensor(hT[:, 4 * half:4 * half + 4, at:at + CB], src[:, :, r * GRID + b * CB:r * GRID + (b + 1) * CB],
                                                     gg.unsqueeze(2).to_broadcast([P, 4, CB]), ALU.mult)
                    last.then_inc(norm_evac, 1)

        x_loaded = sem("x_loaded")
        norm_squares = sem("norm_squares")
        norm_mean = sem("norm_mean")
        norm_root = sem("norm_root")
        norm_rstd = sem("norm_rstd")
        norm_scaled = sem("norm_scaled")
        norm_turned = slots("norm_turned")
        norm_evac = slots("norm_evac")
        rows_stored = sem("rows_stored")

        class Attention:

            def __init__(self, name, carve, bias):
                self.name, self.bias = name, bias
                self.probs = carve(2, 512)
                self.pT = carve(2, 512)
                self.scored = slots(f"{name}_scored")
                self.maxed = slots(f"{name}_maxed")
                self.negated = slots(f"{name}_negated")
                self.exped = slots(f"{name}_exped")
                self.turned = slots(f"{name}_turned_p")
                self.pT_in = slots(f"{name}_pT_in")
                self.summed = slots(f"{name}_summed")
                self.inverted = slots(f"{name}_inverted")
                self.o_out = slots(f"{name}_o_out")
                self.o_turned = slots(f"{name}_o_turned")
                self.o_in = slots(f"{name}_o_in")

            def pe(self, pe, units, u0, t0, q, k, v, o_sb):
                n, tile = len(units), 0
                for j in range(n + 3):
                    if j < n:
                        u = units[j]
                        pe.wait_ge(self.maxed if self.bias else self.exped, after(u0 + j - 2))
                        for i, h in enumerate(u.heads):
                            last = pe.matmul(score_ps[:u.nq, j % 2, u.cols(i)], q(u, h), k(u, h), start=True, stop=True)
                        last.then_inc(self.scored, 1)
                    if 1 <= j <= n:
                        u, b = units[j - 1], (j - 1) % 2
                        pe.wait_ge(self.exped, after(u0 + j - 1))
                        pe.wait_ge(self.pT_in, after(u0 + j - 3))
                        if u.kt < P:
                            settle(pe)
                        for i in range(len(u.heads) * len(u.tiles)):
                            last = pe.transpose(pT_ps[:u.kt, b, i * u.nq:(i + 1) * u.nq],
                                                self.probs[:u.nq, b, i * u.kt:(i + 1) * u.kt], ident[:u.nq, :u.nq])
                        last.then_inc(self.turned, 1)
                    if 2 <= j <= n + 1:
                        u, b = units[j - 2], j % 2
                        pe.wait_ge(self.pT_in, after(u0 + j - 2))
                        pe.wait_ge(self.o_out, after(u0 + j - 3))
                        if u.kt < P:
                            settle(pe)
                        for i, h in enumerate(u.heads):
                            for m, t in enumerate(u.tiles):
                                at = (i * len(u.tiles) + m) * u.nq
                                last = pe.matmul(o_ps[:u.nq, 0, i * HD:(i + 1) * HD],
                                                 self.pT[:u.kt, b, at:at + u.nq], v(u, h, t),
                                                 start=(m == 0), stop=(m == len(u.tiles) - 1))
                        last.then_inc(self.summed, 1)
                    if o_sb is not None and j >= 3 and units[j - 3].last:
                        u, b = units[j - 3], tile % 2
                        pe.wait_ge(self.o_out, after(u0 + j - 3))
                        pe.wait_ge(self.o_in, after(t0 + tile - 1))
                        if u.nq < P:
                            settle(pe)
                        pe.transpose(o_ps[:, 1, :u.nq], o_sb[:u.nq, b], ident[:u.nq, :u.nq]).then_inc(self.o_turned, 1)
                        tile += 1

            def dve(self, dve, units, u0, t0, bias, out, turned_out):
                n, tile, done = len(units), 0, 0
                for j in range(n + 3):
                    if j < n:
                        u, b = units[j], j % 2
                        dve.wait_ge(self.scored, after(u0 + j))
                        if self.bias:
                            dve.wait_ge(self.turned, after(u0 + j - 2))
                            settle(dve)
                            for i, h in enumerate(u.heads):
                                bb = bias(u, h)
                                shape = "p (b r c) -> p b r c" if len(bb.shape) == 4 else None
                                s, o = score_ps[:u.nq, b, u.cols(i)], self.probs[:u.nq, b, u.cols(i)]
                                if shape:
                                    dims = dict(b=bb.shape[1], r=bb.shape[2])
                                    s, o = s.rearrange(shape, **dims), o.rearrange(shape, **dims)
                                elif len(bb.shape) == 3:
                                    s, o = (y.rearrange("p (b c) -> p b c", b=bb.shape[1]) for y in (s, o))
                                last = dve.tensor_tensor_reduce(o, s, bb, 1.0, LOW, ALU.add, ALU.max, smax[:u.nq, j, i:i + 1])
                            last.then_inc(self.maxed, 1)
                            dve.wait_ge(self.maxed, after(u0 + j))
                            dve.tensor_scalar(nmax[:u.nq, j, :len(u.heads)], smax[:u.nq, j, :len(u.heads)], -1.0, None,
                                              ALU.mult).then_inc(self.negated, 1)
                        else:
                            dve.tensor_reduce(nmax[:u.nq, j, :len(u.heads)],
                                              score_ps[:u.nq, b, :u.nk * len(u.heads)].rearrange("p (h k) -> p h k", k=u.nk),
                                              AX.X, ALU.max, negate=True).then_inc(self.negated, 1)
                    if 2 <= j <= n + 1:
                        u = units[j - 2]
                        dve.wait_ge(self.summed, after(u0 + j - 2))
                        out(dve, u, j - 2, u0, t0, done, o_ps[:u.nq, 0, :len(u.heads) * HD])
                        done += u.last
                    if turned_out is not None and j >= 3 and units[j - 3].last:
                        u = units[j - 3]
                        dve.wait_ge(self.o_turned, after(t0 + tile))
                        dve.tensor_copy(turned_out(u), o_ps[:, 1, :u.nq] if len(turned_out(u).shape) == 2 else
                                        o_ps[:, 1, :u.nq].rearrange("p (r c) -> p r c", c=CB)).then_inc(self.o_in, 1)
                        tile += 1

            def normalised(self, o_sb):
                def out(dve, u, j, u0, t0, tile, o):
                    k = len(u.heads)
                    dve.reciprocal(rden[:u.nq, j, :k], den[:u.nq, j, :k]).then_inc(self.inverted, 1)
                    dve.wait_ge(self.o_turned, after(t0 + tile - 2))
                    dve.wait_ge(self.inverted, after(u0 + j))
                    for i, h in enumerate(u.heads):
                        last = dve.tensor_scalar(o_sb[:u.nq, tile % 2, h * HD:(h + 1) * HD], o[:, i * HD:(i + 1) * HD],
                                                 rden[:u.nq, j, i:i + 1], None, ALU.mult)
                    last.then_inc(self.o_out, 1)
                return out

            def act(self, act, units, u0):
                n = len(units)
                for j in range(n + 1):
                    if j < n:
                        u, b = units[j], j % 2
                        act.wait_ge(self.negated, after(u0 + j))
                        if not self.bias:
                            act.wait_ge(self.turned, after(u0 + j - 2))
                        src = self.probs if self.bias else score_ps
                        for i in range(len(u.heads)):
                            last = act.activation(self.probs[:u.nq, b, u.cols(i)], src[:u.nq, b, u.cols(i)], ACT.Exp,
                                                  bias=nmax[:u.nq, j, i:i + 1], accum_out=den[:u.nq, j, i:i + 1])
                        last.then_inc(self.exped, 1)
                    if j >= 1:
                        u, b = units[j - 1], (j - 1) % 2
                        act.wait_ge(self.turned, after(u0 + j - 1))
                        act.wait_ge(self.summed, after(u0 + j - 3))
                        w = len(u.heads) * len(u.tiles) * u.nq
                        act.activation(self.pT[:u.kt, b, :w], pT_ps[:u.kt, b, :w], ACT.Copy).then_inc(self.pT_in, 1)

        class Project:

            def __init__(self, name):
                self.ready = slots(f"{name}_ready")
                self.act_out = slots(f"{name}_act_out")
                self.dve_out = slots(f"{name}_dve_out")

            def pe(self, pe, blocks, h0):
                for n, block in enumerate(blocks):
                    pe.wait_ge(self.dve_out if n % 2 else self.act_out, after(h0 + n // 2 - 1))
                    block(pe, proj_ps[:, n % 2]).then_inc(self.ready, 1)

            def out(self, eng, odd, copies, h0):
                for n in range(odd, len(copies), 2):
                    eng.wait_ge(self.ready, after(2 * h0 + n))
                    copies[n](eng, proj_ps[:, n % 2]).then_inc(self.dve_out if odd else self.act_out, 1)

            def all_out(self, eng, half_blocks):
                eng.wait_ge(self.act_out, after(half_blocks - 1))
                eng.wait_ge(self.dve_out, after(half_blocks - 1))

        def product(out, lhs, rhs, n):
            def block(pe, bank):
                for c in range(n):
                    last = pe.matmul(out(bank), lhs(c), rhs(c), start=(c == 0), stop=(c == n - 1))
                return last
            return block

        def wide(*blocks):
            def block(pe, bank):
                for b in blocks:
                    last = b(pe, bank)
                return last
            return block

        def copy_to(dst, src, scale=None):
            def copy(eng, bank):
                if eng.engine == mybir.EngineType.Activation:
                    return eng.activation(dst, src(bank), ACT.Copy, scale=1.0 if scale is None else scale)
                if scale is None:
                    return eng.tensor_copy(dst, src(bank))
                return eng.tensor_scalar(dst, src(bank), scale, None, ALU.mult)
            return copy

        def split_heads(q, scale):
            def copy(eng, bank):
                for h in range(2):
                    r = slice(h * HD, (h + 1) * HD)
                    last = copy_to(q(h)[r], lambda bank: bank[r, 0:HALF], scale)(eng, bank)
                return last
            return copy

        def cols(a, b, rows=P):
            return lambda bank: bank[:rows, a:b]

        class MixerA:
            def __init__(self):
                c = Carve()
                self.w = c(DC, 768)
                self.q = c(AH, TOK)
                self.k = c(2, TOK)
                self.v = c(8, AH * HD)
                self.bias = [c(AH, 384), c(AH, P), c(AH, P)]
                self.stage = c(2, OROW)
                self.table = c(12)
                self.onehot = c(1024)
                self.f = c(1024)
                self.att = Attention("a", c, bias=True)
                self.groups = c(GROUPS, NT, OROW)
                self.a = c(NT, AH * HD)
                self.tmp = c(NT, AH * HD)
                self.m = c(NT, AH)
                self.wt = c(GROUPS, NT, AH)
                self.dn = c(NT, AH)
                self.t4 = c(NT, AH)
                self.proj = Project("a")
                self.zeroed = sem("a_zeroed")
                self.tabled = sem("a_tabled")
                self.mask_set = sem("a_mask_set")
                self.f_ready = sem("a_f_ready")
                self.f_out = sem("a_f_out")
                self.f_stored = sem("a_f_stored")
                self.shifted = sem("a_shifted")
                self.bias_in = sem("a_bias_in")
                self.w_in = sem("a_w_in")
                self.o_stored = [sem(f"a_o_stored{i}") for i in range(2)]
                self.groups_in = sem("a_groups_in")
                self.chain = sem("a_chain")
                self.joined = sem("a_joined")
                self.turned = slots("a_turned")
                self.turned_in = slots("a_turned_in")
                self.scale = HD ** -0.5
                self.units = [units_a(g) for g in range(GROUPS)]
                self.u0 = [sum(len(u) for u in self.units[:g]) for g in range(GROUPS)]
                self.t0 = [sum(self.tiles(h) for h in range(g)) for g in range(GROUPS)]
                for g in range(GROUPS):
                    assert len(self.units[g]) % 2 == 0 and self.tiles(g) % 2 == 0

            def tiles(self, g):
                return 6 if g == 0 else 8

            def blocks(self, g):
                out = []
                for part in (0, 1):
                    for pair in (0, 1):
                        for s in (0, HALF):
                            at = part * 256 + pair * P
                            out.append(product(cols(0, HALF), lambda c, at=at: self.w[:, c, at:at + P],
                                               lambda c, s=s: hT[:, c, s:s + HALF], DC))
                for ts in self.v_blocks(g):
                    rows = P if g == 0 or ts[0] < 4 else HD
                    out.append(wide(*[product(cols(i * 256, (i + 1) * 256, rows), lambda c, t=t: tokens_a(hT[:, c], g, t),
                                              lambda c: self.w[:, c, 512:768], DC) for i, t in enumerate(ts)]))
                return out

            def v_blocks(self, g):
                return [[0, 1], [2, 3], [4], [5]] if g == 0 else [[0, 1], [2, 3], [4, 5], [6, 7]]

            def copies(self, g):
                out = []
                for pair in (0, 1):
                    for s in (0, HALF):
                        out.append(split_heads(lambda h, pair=pair, s=s: self.q[:, 2 * pair + h, s:s + HALF], self.scale))
                for pair in (0, 1):
                    for s in (0, HALF):
                        out.append(copy_to(self.k[:, pair, s:s + HALF], cols(0, HALF)))
                for ts in self.v_blocks(g):
                    rows = P if g == 0 or ts[0] < 4 else HD
                    out.append(copy_to(self.v[:rows, ts[0]:ts[-1] + 1].rearrange("p t n -> p (t n)"), cols(0, 256 * len(ts), rows)))
                return out

            def half(self, g):
                return 6 * g

            def q_of(self, g):
                return lambda u, h: tokens_a(self.q[:, h], g, u.tile)

            def k_of(self, g):
                def k(u, h):
                    ap = self.k[:, h // 2]
                    if g == 0:
                        return ap[:, u.tiles[0] * P:(u.tiles[-1] + 1) * P]
                    return tokens_a(ap, g, u.tile)
                return k

            def bias_of(self, g):
                def bias(u, h):
                    if g == 0:
                        at = P if u.first_key == 0 else 0
                        return self.bias[0][:u.nq, h, at:at + u.nk]
                    return self.bias[g][:u.nq, h, :u.nk]
                return bias

            def sp(self, sp):
                sp.dma_start(self.table[0:32, :], t5).then_inc(self.tabled, 16)
                sp.dma_start(self.onehot[0:33, :], onehot).then_inc(self.tabled, 16)
                sp.dma_start(self.w, w_a[0]).then_inc(self.w_in, 16)
                sp.wait_ge(self.f_out, 2)
                sp.dma_start(f_dram, self.f[0:12, :]).then_inc(self.f_stored, 16)
                sp.wait_ge(self.f_stored, 16)
                with sp.Fori(0, CB) as b:
                    sp.dma_start(shifted_dram[b], f_dram[:, bass.ds(CB - 1 - b, 1024 - CB)]).then_inc(self.shifted, 16)
                sp.wait_ge(self.shifted, 16 * CB)
                for g, (at, n) in enumerate(((0, 384), (512, P), (768, P))):
                    for a in range(P // CB):
                        first = at + P - CB - CB * a
                        sp.dma_start(self.bias[g][a * CB:(a + 1) * CB], shifted_dram[:, AH * g:AH * (g + 1), first:first + n]
                                     ).then_inc(self.bias_in, 16)
                for g in range(GROUPS):
                    if g:
                        sp.wait_ge(self.proj.ready, after(12 * g - 1))
                        sp.dma_start(self.w, w_a[g]).then_inc(self.w_in, 16)
                    tile = 0
                    for j, u in enumerate(self.units[g]):
                        if not u.last:
                            continue
                        sp.wait_ge(self.att.o_out, after(self.u0[g] + j))
                        rows = oa_dram[g].rearrange("t n -> n t")
                        dst = tokens_a(rows, g, u.tile)
                        dst = dst.rearrange("n t -> t n")
                        sp.dma_start(dst, self.stage[:u.nq, tile % 2]).then_inc(self.o_stored[tile % 2], 16)
                        tile += 1

            def stored(self, eng, tiles):
                for par in range(2):
                    if (n := (tiles + 1 - par) // 2) > 0:
                        eng.wait_ge(self.o_stored[par], 16 * n)

            def out_of(self, g):
                def out(dve, u, j, u0, t0, tile, o):
                    k, h0, s = len(u.heads), u.heads[0], self.stage[:u.nq, tile % 2].rearrange("p (h c) -> p h c", h=AH)
                    n = self.t0[g] + tile
                    if n >= 2:
                        dve.wait_ge(self.o_stored[tile % 2], 16 * (n // 2))
                    dve.tensor_copy(s[:, h0:h0 + k, HD], smax[:u.nq, j, :k])
                    dve.tensor_copy(s[:, h0:h0 + k, HD + 1], den[:u.nq, j, :k])
                    dve.tensor_copy(s[:, h0:h0 + k, 0:HD], o.rearrange("p (h c) -> p h c", h=k)).then_inc(self.att.o_out, 1)
                return out

            def pe(self, pe):
                pe.wait_ge(self.tabled, 32)
                pe.wait_ge(self.mask_set, 1)
                for b in range(2):
                    pe.matmul(score_ps[0:12, b, :], self.table[0:33, :], self.onehot[0:33, b * 512:(b + 1) * 512],
                              start=True, stop=True).then_inc(self.f_ready, 1)
                pe.wait_ge(self.f_out, 2)
                for g in range(GROUPS):
                    pe.wait_ge(self.w_in, 16 * (g + 1))
                    self.proj.pe(pe, self.blocks(g), self.half(g))
                    self.proj.all_out(pe, self.half(g) + 6)
                    v = lambda u, h, t: self.v[:u.kt, t, h * HD:(h + 1) * HD]
                    self.att.pe(pe, self.units[g], self.u0[g], self.t0[g], self.q_of(g), self.k_of(g), v, None)

            def act(self, act):
                act.wait_ge(self.zeroed, 1)
                for g in range(GROUPS):
                    self.proj.out(act, 0, self.copies(g), self.half(g))
                    self.att.act(act, self.units[g], self.u0[g])

            def dve(self, dve):
                dve.memset(self.table[32:33, :], MASKED).then_inc(self.mask_set, 1)
                dve.memset(self.q, 0.0).then_inc(self.zeroed, 1)
                dve.wait_ge(self.zeroed, 1)
                for b in range(2):
                    dve.wait_ge(self.f_ready, b + 1)
                    dve.tensor_copy(self.f[0:12, b * 512:(b + 1) * 512], score_ps[0:12, b, :]).then_inc(self.f_out, 1)
                for g in range(GROUPS):
                    self.proj.out(dve, 1, self.copies(g), self.half(g))
                    if g == 0:
                        dve.wait_ge(self.bias_in, 16 * GROUPS * (P // CB))
                    self.att.dve(dve, self.units[g], self.u0[g], self.t0[g], self.bias_of(g), self.out_of(g), None)

            def join_sp(self, sp):
                for g in range(GROUPS):
                    sp.dma_start(self.groups[:, g], oa_dram[g].rearrange("(t p) n -> p t n", p=P)).then_inc(self.groups_in, 16)

            def join_dve(self, dve):
                steps = [0]

                def step(ins):
                    steps[0] += 1
                    ins.then_inc(self.chain, 1)
                    dve.wait_ge(self.chain, steps[0])

                dve.wait_ge(self.groups_in, 16 * GROUPS)
                g = [self.groups[:, i].rearrange("p t (h c) -> p t h c", h=AH) for i in range(GROUPS)]
                step(dve.tensor_tensor(self.m, g[0][:, :, :, HD], g[1][:, :, :, HD], ALU.max))
                step(dve.tensor_tensor(self.m, self.m, g[2][:, :, :, HD], ALU.max))
                for i in range(GROUPS):
                    step(dve.tensor_tensor(self.wt[:, i], g[i][:, :, :, HD], self.m, ALU.subtract))
                dve.tensor_copy(self.t4, self.m).then_inc(self.joined, 1)
                dve.wait_ge(self.joined, 2)
                step(dve.tensor_tensor(self.dn, self.wt[:, 0], g[0][:, :, :, HD + 1], ALU.mult))
                for i in (1, 2):
                    step(dve.tensor_tensor(self.t4, self.wt[:, i], g[i][:, :, :, HD + 1], ALU.mult))
                    step(dve.tensor_tensor(self.dn, self.dn, self.t4, ALU.add))
                step(dve.reciprocal(self.dn, self.dn))
                for i in range(GROUPS):
                    step(dve.tensor_tensor(self.wt[:, i], self.wt[:, i], self.dn, ALU.mult))
                for t in range(NT):
                    a = self.a[:, t].rearrange("p (h c) -> p h c", h=AH)
                    tmp = self.tmp[:, t].rearrange("p (h c) -> p h c", h=AH)
                    w = [self.wt[:, i, t].unsqueeze(2).to_broadcast([P, AH, HD]) for i in range(GROUPS)]
                    step(dve.tensor_tensor(a, g[0][:, t, :, 0:HD], w[0], ALU.mult))
                    for i in (1, 2):
                        step(dve.tensor_tensor(tmp, g[i][:, t, :, 0:HD], w[i], ALU.mult))
                        step(dve.tensor_tensor(a, a, tmp, ALU.add))
                dve.sem_inc(self.joined, 1)
                for t in range(NT):
                    dve.wait_ge(self.turned, after(t))
                    dve.tensor_copy(aT[:, 0:2, t * P:(t + 1) * P],
                                    proj_ps[:, t % 2, 0:256].rearrange("p (c t) -> p c t", c=2)).then_inc(self.turned_in, 1)

            def join_act(self, act):
                act.wait_ge(self.joined, 1)
                act.activation(self.wt, self.wt, ACT.Exp).then_inc(self.joined, 1)

            def join_pe(self, pe):
                pe.wait_ge(self.joined, 3)
                for t in range(NT):
                    pe.wait_ge(self.turned_in, after(t - 2))
                    for c in range(2):
                        last = pe.transpose(proj_ps[:, t % 2, c * P:(c + 1) * P], self.a[:, t, c * P:(c + 1) * P], ident[:])
                    last.then_inc(self.turned, 1)

        class MixerB:
            def __init__(self):
                c = Carve()
                self.w = c(DC, B_IN)
                self.u = c(NT, B_IN)
                self.junk = c(QR)
                self.kk = c(NT, P)
                self.rope = c(NT, 2, ROPE // 2)
                self.rt = c(4, NT, ROPE // 2)
                self.cq = c(3, TOK)
                self.ckv = c(2, TOK)
                self.wq = c(3, 256)
                self.wkv = c(2, 256)
                self.q_table = c(TOK)
                self.q = c(2, TOK)
                self.k = c(2, TOK)
                self.v = c(NT, P)
                self.o_sb = c(2, P)
                self.att = Attention("b", c, bias=False)
                self.proj = Project("b")
                self.lat = Project("b_latent")
                self.units = units_b()
                self.tiles = NT
                self.w_in = sem("b_w_in")
                self.tables_in = sem("b_tables_in")
                self.squares = sem("b_squares")
                self.mean = sem("b_mean")
                self.chain = sem("b_chain")
                self.scaled = sem("b_scaled")
                self.turned = slots("b_turned")
                self.turned_act = slots("b_turned_act")
                self.turned_dve = slots("b_turned_dve")
                self.pair_in = sem("b_pair_in")
                self.v_blocks = [[0, 1, 2], [3, 4, 5]]

            def latent_blocks(self):
                return [product(cols(0, n), lambda c, t=t: hT[:, c, t * P:(t + 1) * P], lambda c, a=a, n=n: self.w[:, c, a:a + n], DC)
                        for t in range(NT) for a, n in ((0, QR), (QR, KVR + ROPE))]

            def latent_copies(self):
                return [copy_to(self.u[:, t, a:a + n], cols(0, n)) for t in range(NT) for a, n in ((0, QR), (QR, KVR + ROPE))]

            def blocks(self):
                halves = (0, HALF)
                q = [product(cols(0, HALF), lambda c, h=h: self.wq[:, c, h * P:(h + 1) * P],
                             lambda c, s=s: self.cq[:, c, s:s + HALF], 3) for h in (0, 1) for s in halves]
                k = [product(cols(0, HALF), lambda c: self.wkv[:, c, 0:P], lambda c, s=s: self.ckv[:, c, s:s + HALF], 2) for s in halves]
                v = [wide(*[product(cols(i * P, (i + 1) * P), lambda c, t=t: self.ckv[:, c, t * P:(t + 1) * P],
                                    lambda c: self.wkv[:, c, P:2 * P], 2) for i, t in enumerate(ts)]) for ts in self.v_blocks]
                return [k[0], q[0], k[1], q[1], v[0], q[2], v[1], q[3]]

            def copies(self):
                def k_copy(s):
                    def copy(act, bank):
                        act.activation(self.k[0:HD, 0, s:s + HALF], bank[0:HD, 0:HALF], ACT.Copy)
                        return act.activation(self.k[0:HD, 1, s:s + HALF], bank[HD:P, 0:HALF], ACT.Copy)
                    return copy

                def q_copy(h, s):
                    return lambda dve, bank: dve.tensor_tensor(self.q[:, h, s:s + HALF], bank[:, 0:HALF],
                                                               self.q_table[:, s:s + HALF], ALU.mult)
                v = [copy_to(self.v[:, ts[0]:ts[-1] + 1].rearrange("p t n -> p (t n)"), cols(0, HALF)) for ts in self.v_blocks]
                return [k_copy(0), q_copy(0, 0), k_copy(HALF), q_copy(0, HALF), v[0], q_copy(1, 0), v[1], q_copy(1, HALF)]

            def sp(self, sp):
                sp.dma_start(self.w, w_b).then_inc(self.w_in, 16)
                sp.dma_start(self.q_table, q_table).then_inc(self.tables_in, 16)
                sp.dma_start(self.rope, rope_in).then_inc(self.tables_in, 16)
                sp.dma_start(self.wq, w_qb[0]).then_inc(self.pair_in, 16)
                sp.dma_start(self.wkv, w_kvb[0]).then_inc(self.pair_in, 16)
                with sp.Fori(1, B_PAIRS) as i:
                    sp.wait_ge(self.proj.ready, after(8 * i - 1))
                    sp.dma_start(self.wq, w_qb[i]).then_inc(self.pair_in, 16)
                    sp.dma_start(self.wkv, w_kvb[i]).then_inc(self.pair_in, 16)

            def pe(self, pe):
                pe.wait_ge(self.w_in, 16)
                self.lat.pe(pe, self.latent_blocks(), 0)
                pe.wait_ge(self.scaled, 1)
                for t in range(NT):
                    for part in range(2):
                        pe.wait_ge((self.turned_act, self.turned_dve)[part], after(t - 1))
                        srcs = [self.u[:, t, c * P:(c + 1) * P] for c in range(3)] + [self.kk[:, t]] if part == 0 else \
                               [self.u[:, t, QR + c * P:QR + (c + 1) * P] for c in range(2)]
                        for i, s in enumerate(srcs):
                            last = pe.transpose(proj_ps[:, part, i * P:(i + 1) * P], s, ident[:])
                        last.then_inc(self.turned, 1)
                pe.wait_ge(self.turned_act, after(NT - 1))
                pe.wait_ge(self.turned_dve, after(NT - 1))
                with pe.Fori(0, B_PAIRS) as i:
                    pe.wait_ge(self.pair_in, 32 * i + 32)
                    self.proj.pe(pe, self.blocks(), 4 * i)
                    self.proj.all_out(pe, 4 * i + 4)
                    v = lambda u, h, t: self.v[:, t, h * HD:(h + 1) * HD]
                    self.att.pe(pe, self.units, len(self.units) * i, self.tiles * i,
                                lambda u, h: self.q[:, h, u.tile * P:(u.tile + 1) * P],
                                lambda u, h: self.k[:, h, u.tiles[0] * P:(u.tiles[-1] + 1) * P], v, self.o_sb)

            def act(self, act):
                self.lat.out(act, 0, self.latent_copies(), 0)
                act.wait_ge(self.lat.dve_out, after(NT - 1))
                for t in range(NT):
                    for i, (a, n) in enumerate(((0, QR), (QR, KVR))):
                        if 2 * t + i:
                            act.wait_ge(self.squares, 2 * t + i)
                        act.activation(self.junk[:, :n], self.u[:, t, a:a + n], ACT.Square,
                                       accum_out=bstat[:, i, t:t + 1]).then_inc(self.squares, 1)
                act.wait_ge(self.mean, 1)
                act.activation(brstd[:], brstd[:], ACT.Sqrt).then_inc(self.mean, 1)
                for t in range(NT):
                    act.wait_ge(self.turned, after(2 * t))
                    for c in range(3):
                        last = act.activation(self.cq[:, c, t * P:(t + 1) * P], proj_ps[:, 0, c * P:(c + 1) * P], ACT.Copy,
                                              scale=gq[:, c:c + 1])
                    for h in range(2):
                        last = act.activation(self.k[HD:P, h, t * P:(t + 1) * P], proj_ps[HD:P, 0, 3 * P:4 * P], ACT.Copy)
                    last.then_inc(self.turned_act, 1)
                with act.Fori(0, B_PAIRS) as i:
                    self.proj.out(act, 0, self.copies(), 4 * i)
                    self.att.act(act, self.units, len(self.units) * i)

            def dve(self, dve):
                dve.memset(self.kk, 0.0)
                self.lat.out(dve, 1, self.latent_copies(), 0)
                steps = [0]

                def step(ins):
                    steps[0] += 1
                    ins.then_inc(self.chain, 1)
                    dve.wait_ge(self.chain, steps[0])

                dve.wait_ge(self.squares, 2 * NT)
                dve.tensor_scalar(brstd[:, 0], bstat[:, 0], 1.0 / QR, EPS, ALU.mult, ALU.add)
                dve.tensor_scalar(brstd[:, 1], bstat[:, 1], 1.0 / KVR, EPS, ALU.mult, ALU.add).then_inc(self.mean, 1)
                dve.wait_ge(self.mean, 2)
                step(dve.reciprocal(brstd[:], brstd[:]))
                dve.wait_ge(self.tables_in, 32)
                R = ROPE // 2
                k1, k2 = self.u[:, :, QR + KVR:QR + KVR + R], self.u[:, :, QR + KVR + R:B_IN]
                cos, sin = self.rope[:, :, 0], self.rope[:, :, 1]
                for i, (a, b) in enumerate(((k1, cos), (k2, sin), (k2, cos), (k1, sin))):
                    last = dve.tensor_tensor(self.rt[:, i], a, b, ALU.mult)
                step(last)
                for twice in range(2):
                    at = HD + twice * ROPE
                    dve.tensor_tensor(self.kk[:, :, at:at + R], self.rt[:, 0], self.rt[:, 1], ALU.subtract)
                    dve.tensor_tensor(self.kk[:, :, at + R:at + 2 * R], self.rt[:, 2], self.rt[:, 3], ALU.add)
                for t in range(NT):
                    for i, (a, n) in enumerate(((0, QR), (QR, KVR))):
                        last = dve.tensor_scalar(self.u[:, t, a:a + n], self.u[:, t, a:a + n], brstd[:, i, t:t + 1], None, ALU.mult)
                last.then_inc(self.scaled, 1)
                for t in range(NT):
                    dve.wait_ge(self.turned, after(2 * t + 1))
                    dve.tensor_tensor(self.ckv[:, :, t * P:(t + 1) * P], proj_ps[:, 1, 0:256].rearrange("p (c t) -> p c t", c=2),
                                      gkv.unsqueeze(2).to_broadcast([P, 2, P]), ALU.mult).then_inc(self.turned_dve, 1)
                with dve.Fori(0, B_PAIRS) as i:
                    self.proj.out(dve, 1, self.copies(), 4 * i)
                    self.att.dve(dve, self.units, len(self.units) * i, self.tiles * i, None, self.att.normalised(self.o_sb),
                                 lambda u: aT[:, i + 2, u.tile * P:(u.tile + 1) * P])

        class MixerC:
            def __init__(self):
                c = Carve()
                self.w = c(DC, 384)
                self.q = c(2, TOK)
                self.k = c(TOK)
                self.v = c(2 * NB, P)
                self.window = c(2, C_ROWS, WIN)
                self.bias = c(2, 7, C_ROWS, CB)
                self.mask = c(7, CB)
                self.o_sb = c(2, P)
                self.att = Attention("c", c, bias=True)
                self.proj = Project("c")
                self.zeroed = sem("c_zeroed")
                self.units = units_c()
                self.tiles = 2 * NB
                self.windows_out = sem("c_windows_out")
                self.mask_in = sem("c_mask_in")
                self.w_in = sem("c_w_in")
                self.window_in = sem("c_window_in")
                self.biased = slots("c_biased")
                self.scale = HD ** -0.5
                assert len(self.units) == 10

            def windows(self, sp):
                with sp.Fori(0, CB) as c:
                    sp.dma_start(window_dram[c], rpb[:, :, bass.ds(CB - 1 - c, WIN)]).then_inc(self.windows_out, 16)

            def blocks(self):
                out = [product(cols(0, HALF), lambda c, a=a: self.w[:, c, a:a + P], lambda c, s=s: hT[:, c, s:s + HALF], DC)
                       for a in (0, P) for s in (0, HALF)]
                for ts in (range(0, NB), range(NB, 2 * NB)):
                    rows = P if ts[0] == 0 else CB * S_ROWS
                    out.append(wide(*[product(cols(i * P, (i + 1) * P, rows), lambda c, t=t: run_c(hT[:, c], t),
                                              lambda c: self.w[:, c, 256:384], DC) for i, t in enumerate(ts)]))
                return out

            def copies(self):
                out = [split_heads(lambda h, s=s: self.q[:, h, s:s + HALF], self.scale) for s in (0, HALF)]
                out += [copy_to(self.k[:, s:s + HALF], cols(0, HALF)) for s in (0, HALF)]
                out.append(copy_to(self.v[:, 0:NB].rearrange("p t n -> p (t n)"), cols(0, 512)))
                rows = CB * S_ROWS
                out.append(copy_to(self.v[:rows, NB:2 * NB].rearrange("p t n -> p (t n)"), cols(0, 512, rows)))
                return out

            def sp(self, sp):
                sp.wait_ge(self.windows_out, 16 * CB)
                sp.dma_start(self.mask, col_mask).then_inc(self.mask_in, 16)
                with sp.Fori(0, C_PAIRS) as i:
                    sp.wait_ge(self.proj.ready, after(6 * i - 1))
                    sp.dma_start(self.w, w_c[i]).then_inc(self.w_in, 16)
                    sp.wait_ge(self.biased, after(i - 1))
                    for r in range(C_ROWS):
                        sp.dma_start(self.window[r * CB:(r + 1) * CB], window_dram[:, bass.ds(2 * i, 2), C_ROWS - 1 - r:2 * C_ROWS - 1 - r]
                                     ).then_inc(self.window_in, 16)

            def pool(self, pool):
                pool.wait_ge(self.mask_in, 16)
                with pool.Fori(0, C_PAIRS) as i:
                    pool.wait_ge(self.window_in, 16 * C_ROWS * i + 16 * C_ROWS)
                    pool.wait_ge(self.att.maxed, after(len(self.units) * i - 1))
                    for h in range(2):
                        win = self.window[:, h].rearrange("p r (b c) -> p b r c", c=CB)
                        for b0, n, d0 in ((0, 2, 1), (2, 3, 0), (5, 2, 0)):
                            last = pool.tensor_tensor(self.bias[:, h, b0:b0 + n], win[:, d0:d0 + n],
                                                      self.mask[:, b0:b0 + n].unsqueeze(2).to_broadcast([P, n, C_ROWS, CB]), ALU.add)
                    last.then_inc(self.biased, 1)

            def bias_of(self, u, h):
                at, n = C_BIAS0[u.first_key], len(u.tiles)
                if u.tile < NB:
                    return self.bias[:, h, at:at + n].rearrange("p b r c -> p (b r c)")
                return self.bias[:u.nq, h, at:at + n, 0:S_ROWS].rearrange("p b r c -> p b (r c)")

            def pe(self, pe):
                with pe.Fori(0, C_PAIRS) as i:
                    pe.wait_ge(self.w_in, 16 * i + 16)
                    self.proj.pe(pe, self.blocks(), 3 * i)
                    self.proj.all_out(pe, 3 * i + 3)
                    v = lambda u, h, t: self.v[:u.kt, t, h * HD:(h + 1) * HD]
                    self.att.pe(pe, self.units, len(self.units) * i, self.tiles * i,
                                lambda u, h: run_c(self.q[:, h], u.tile),
                                lambda u, h: run_c(self.k, u.tiles[0], len(u.tiles)), v, self.o_sb)

            def act(self, act):
                act.wait_ge(self.zeroed, 1)
                with act.Fori(0, C_PAIRS) as i:
                    self.proj.out(act, 0, self.copies(), 3 * i)
                    self.att.act(act, self.units, len(self.units) * i)

            def dve(self, dve):
                dve.memset(self.q, 0.0).then_inc(self.zeroed, 1)
                dve.wait_ge(self.zeroed, 1)
                with dve.Fori(0, C_PAIRS) as i:
                    self.proj.out(dve, 1, self.copies(), 3 * i)
                    dve.wait_ge(self.biased, after(i))
                    self.att.dve(dve, self.units, len(self.units) * i, self.tiles * i, self.bias_of, self.att.normalised(self.o_sb),
                                 lambda u: tokens_c(aT[:, i], u.tile))

        class OutProject:
            def __init__(self, l):
                self.l = l
                self.w = Carve(ARENA - DC * D)(DC, D)

            def sp(self, sp):
                sp.dma_start(self.w, w_out[self.l]).then_inc(out_w_in, 16)

            def pe(self, pe):
                pe.wait_ge(out_w_in, 16 * (self.l + 1))
                for n in range(2 * NT):
                    t, half = n // 2, n % 2
                    pe.wait_ge(out_added, after(2 * NT * self.l + n - 2))
                    for c in range(DC):
                        last = pe.matmul(proj_ps[:, half], aT[:, c, t * P:(t + 1) * P], self.w[:, c, half * 512:(half + 1) * 512],
                                         start=(c == 0), stop=(c == DC - 1))
                    last.then_inc(out_ready, 1)

            def dve(self, dve):
                for n in range(2 * NT):
                    t, half = n // 2, n % 2
                    dve.wait_ge(out_ready, after(2 * NT * self.l + n))
                    xs = x[:, t, half * 512:(half + 1) * 512]
                    dve.tensor_tensor(xs, xs, proj_ps[:, half], ALU.add).then_inc(out_added, 1)

        out_w_in = sem("out_w_in")
        out_ready = slots("out_ready")
        out_added = slots("out_added")

        class Route:
            def __init__(self, l):
                self.l = l
                c = Carve(3 * DC * FF)
                self.z = c(NT, NE)
                self.z2 = c(NT, NE)
                self.m = c(NT)
                self.affT = c(TOK)
                self.work = c(TOK)
                self.vals = c(CAP)
                self.idx = c(CAP).bitcast(U32)
                self.idx_f = c(CAP)
                self.idxT = idxT[:, NE * l:NE * l + NE]
                self.gateT = gateT[:, NE * l:NE * l + NE]
            def pe(self, pe):
                for t in range(NT):
                    for c in range(DC):
                        last = pe.matmul(proj_ps[:, 0, t * NE:(t + 1) * NE], hT[:, c, t * P:(t + 1) * P], router_sb[:, self.l, c],
                                         start=(c == 0), stop=(c == DC - 1))
                last.then_inc(route_logits, 1)
                pe.wait_ge(route_aff, self.l + 1)
                for t in range(NT):
                    last = pe.transpose(score_ps[:NE, t // 4, (t % 4) * P:(t % 4 + 1) * P], self.z[:, t], ident[:])
                last.then_inc(route_turned, 1)
                pe.wait_ge(route_chosen, self.l + 1)
                pe.transpose(proj_ps[:CAP, 1, 0:NE], self.idx_f[:NE, :], ident[:NE, :NE])
                pe.transpose(proj_ps[:CAP, 1, NE:2 * NE], self.vals[:NE, :], ident[:NE, :NE]).then_inc(route_lists, 1)

            def act(self, act):
                act.wait_ge(route_exped, 2 * self.l + 1)
                act.activation(self.z2, self.z2, ACT.Exp).then_inc(route_exped, 1)

            def dve(self, dve):
                steps = [0]

                def step(ins):
                    steps[0] += 1
                    ins.then_inc(route_chain, 1)
                    dve.wait_ge(route_chain, steps[0] + STEPS * self.l)

                dve.wait_ge(route_logits, self.l + 1)
                z = proj_ps[:, 0, 0:NT * NE].rearrange("p (t e) -> p t e", e=NE)
                wide_m = self.m.unsqueeze(2).to_broadcast([P, NT, NE])
                step(dve.tensor_reduce(self.m, z, AX.X, ALU.max))
                dve.tensor_tensor(self.z2, z, wide_m, ALU.subtract).then_inc(route_exped, 1)
                dve.wait_ge(route_exped, 2 * self.l + 2)
                step(dve.tensor_reduce(self.m, self.z2, AX.X, ALU.add))
                step(dve.reciprocal(self.m, self.m))
                dve.tensor_tensor(self.z, self.z2, wide_m, ALU.mult).then_inc(route_aff, 1)
                dve.wait_ge(route_turned, self.l + 1)
                step(dve.tensor_copy(self.work[:NE, 0:PROMPT], score_ps[:NE, 0]))
                step(dve.tensor_copy(self.work[:NE, PROMPT:TOK], score_ps[:NE, 1, 0:SAMPLE]))
                for first, n, at, cap in ((0, PROMPT, 0, CAP_P), (PROMPT, SAMPLE, CAP_P, CAP_S)):
                    left = self.work[:NE, first:first + n]
                    for r in range(at, at + cap, 8):
                        step(dve.max(self.vals[:NE, r:r + 8], left))
                        step(dve.max_index(self.idx[:NE, r:r + 8], self.vals[:NE, r:r + 8], left))
                        if r + 8 < at + cap:
                            step(dve.match_replace(left, self.vals[:NE, r:r + 8], left, -1.0))
                dve.tensor_copy(self.idx_f[:NE, 0:CAP_P], self.idx[:NE, 0:CAP_P])
                dve.tensor_scalar(self.idx_f[:NE, CAP_P:CAP], self.idx[:NE, CAP_P:CAP], float(PROMPT), None, ALU.add).then_inc(route_chosen, 1)
                dve.wait_ge(route_lists, self.l + 1)
                dve.tensor_copy(self.idxT[:CAP, :], proj_ps[:CAP, 1, 0:NE]).then_inc(route_lists_out, 1)
                dve.tensor_copy(self.gateT[:CAP, :], proj_ps[:CAP, 1, NE:2 * NE]).then_inc(route_lists_out, 1)
                assert steps[0] == STEPS

        STEPS = 5 + 3 * (CAP // 8) - 2
        route_logits, route_exped, route_aff = sem("route_logits"), sem("route_exped"), sem("route_aff")
        route_turned, route_chosen, route_lists = sem("route_turned"), sem("route_chosen"), sem("route_lists")
        route_chain, route_lists_out = sem("route_chain"), sem("route_lists_out")

        idxT = sb("idxT", [P, 2 * NE], U32)
        gateT = sb("gateT", [P, 2 * NE])

        SL = 2
        NS = DC // SL

        class Experts:

            def __init__(self):
                n = "moe"
                c = Carve()
                self.w = [c(DC, FF), c(DC, FF), c(DC, D)]
                self.xe = c(D)
                self.silu = c(DC, CAP)
                self.hidT = c(DC, CAP)
                self.yT = c(DC, CAP)
                self.y = c(D)
                self.xeT = c(DC, CAP)
                self.gather_idx = sb(f"{n}_gather_idx", [P, 1], U32)
                self.scatter_idx = sb(f"{n}_scatter_idx", [P, 1], U32)
                self.w_in = [[sem(f"{n}_{m}_in{s}") for s in range(NS)] for m in ("gate", "up", "down")]
                self.used = [slots(f"{n}_{m}_used") for m in ("gate", "up", "down")]
                self.listed = sem(f"{n}_listed")
                self.relisted = sem(f"{n}_relisted")
                self.gathered = sem(f"{n}_gathered")
                self.x_turned = slots(f"{n}_x_turned")
                self.x_in = slots(f"{n}_x_in")
                self.silued = slots(f"{n}_silued")
                self.hidden = slots(f"{n}_hidden")
                self.yT_in = slots(f"{n}_yT_in")
                self.y_turned = slots(f"{n}_y_turned")
                self.y_out = slots(f"{n}_y_out")
                self.scattered = sem(f"{n}_scattered")

            def load(self, sp, m, e, s, wait):
                src = (w_gate, w_up, w_down)[m].rearrange("l e k n -> (l e) k n")
                if wait:
                    sp.wait_ge(self.used[m], after((e - 1) * NS + s))
                sp.dma_start(self.w[m][:, s * SL:(s + 1) * SL],
                             src[e, s * SL * P:(s + 1) * SL * P, :].rearrange("(c p) n -> p c n", p=P)).then_inc(self.w_in[m][s], 16)

            def sp_first(self, l):
                def f(sp):
                    for m in (0, 1):
                        for s in range(NS):
                            self.load(sp, m, NE * l, s, l > 0)
                return f

            def sp(self, l):
                def f(sp):
                    e0, e1 = NE * l, NE * l + NE
                    for m, e in ((0, e0 + 1), (1, e0 + 1), (2, e0)):
                        for s in range(NS):
                            self.load(sp, m, e, s, m < 2 or l > 0)
                    with sp.Fori(e0 + 2, e1) as e:
                        for m, d in ((0, 0), (1, 0), (2, -1)):
                            for s in range(NS):
                                self.load(sp, m, e + d, s, True)
                    for s in range(NS):
                        self.load(sp, 2, e1 - 1, s, True)
                return f

            def pe_product(self, pe, m, e, bank, rhs):
                for s in range(NS):
                    pe.wait_ge(self.w_in[m][s], 16 * e + 16)
                    for c in range(s * SL, (s + 1) * SL):
                        for o in range(DC):
                            last = pe.matmul(bank[:, o // 4, (o % 4) * CAP:(o % 4 + 1) * CAP], self.w[m][:, c, o * P:(o + 1) * P], rhs[:, c],
                                             start=(c == 0 and o % 4 == 0), stop=(c == DC - 1 and o % 4 == 3))
                    last.then_inc(self.used[m], 1)

            def pe_turn_x(self, pe, e, y_before):
                pe.wait_ge(self.gathered, 16 * e + 16)
                if y_before:
                    pe.wait_ge(self.y_out, after(e - 3))
                settle(pe)
                for c in range(DC):
                    last = pe.transpose(o_ps[:, c // 4, (c % 4) * CAP:(c % 4 + 1) * CAP], self.xe[:CAP, c * P:(c + 1) * P], ident[:CAP, :CAP])
                last.then_inc(self.x_turned, 1)

            def pe_gate(self, pe, e):
                pe.wait_ge(self.x_in, after(e))
                pe.wait_ge(self.silued, after(e - 1))
                self.pe_product(pe, 0, e, proj_ps, self.xeT)

            def pe_up(self, pe, e):
                pe.wait_ge(self.hidden, after(e - 1))
                self.pe_product(pe, 1, e, score_ps, self.xeT)

            def pe_down(self, pe, e):
                pe.wait_ge(self.hidden, after(e))
                pe.wait_ge(self.yT_in, after(e - 1))
                self.pe_product(pe, 2, e, pT_ps, self.hidT)

            def pe_turn_y(self, pe, e):
                pe.wait_ge(self.yT_in, after(e))
                pe.wait_ge(self.y_out, after(e - 1))
                settle(pe)
                for c in range(DC):
                    last = pe.transpose(o_ps[:CAP, c // 4, (c % 4) * P:(c % 4 + 1) * P], self.yT[:, c], ident[:])
                last.then_inc(self.y_turned, 1)

            def pe(self, l):
                def f(pe):
                    e0, e1 = NE * l, NE * l + NE
                    self.pe_turn_x(pe, e0, False)
                    self.pe_gate(pe, e0)
                    self.pe_up(pe, e0)
                    self.pe_turn_x(pe, e0 + 1, False)
                    self.pe_gate(pe, e0 + 1)
                    self.pe_up(pe, e0 + 1)
                    self.pe_turn_x(pe, e0 + 2, False)
                    self.pe_down(pe, e0)
                    with pe.Fori(e0 + 2, e1 - 1) as e:
                        self.pe_gate(pe, e)
                        self.pe_turn_y(pe, e - 2)
                        self.pe_up(pe, e)
                        self.pe_turn_x(pe, e + 1, True)
                        self.pe_down(pe, e - 1)
                    self.pe_gate(pe, e1 - 1)
                    self.pe_turn_y(pe, e1 - 3)
                    self.pe_up(pe, e1 - 1)
                    self.pe_down(pe, e1 - 2)
                    self.pe_turn_y(pe, e1 - 2)
                    self.pe_down(pe, e1 - 1)
                    self.pe_turn_y(pe, e1 - 1)
                return f

            def act(self, l):
                def f(act):
                    e0, e1 = NE * l, NE * l + NE
                    self.act_silu(act, e0)
                    self.act_silu(act, e0 + 1)
                    self.act_silu(act, e0 + 2)
                    self.act_y(act, e0, l == 0)
                    with act.Fori(e0 + 3, e1) as e:
                        self.act_silu(act, e)
                        self.act_y(act, e - 2)
                    self.act_y(act, e1 - 2)
                    self.act_y(act, e1 - 1)
                return f

            def act_silu(self, act, e):
                act.wait_ge(self.used[0], after(NS * e + NS - 1))
                act.wait_ge(self.hidden, after(e - 1))
                act.activation(self.silu.rearrange("p (b c) t -> p b (c t)", b=2), proj_ps[:, :, 0:4 * CAP], ACT.Silu).then_inc(self.silued, 1)

            def act_y(self, act, e, first=False):
                act.wait_ge(self.y_turned, after(e))
                if not first:
                    act.wait_ge(self.scattered, 16 * e)
                gate = gateT[:CAP, bass.ds(e, 1)]
                act.activation(self.y[:CAP, :], o_ps[:CAP].rearrange("p b n -> p (b n)"), ACT.Copy, scale=gate).then_inc(self.y_out, 1)

            def dve_x(self, dve, l, e):
                dve.wait_ge(self.x_turned, after(e))
                g = g_of[f"ffn{l}"]
                for half in range(2):
                    last = dve.tensor_tensor(self.xeT[:, 4 * half:4 * half + 4], o_ps[:, half, 0:4 * CAP].rearrange("p (c t) -> p c t", c=4),
                                             g[:, 4 * half:4 * half + 4].unsqueeze(2).to_broadcast([P, 4, CAP]), ALU.mult)
                last.then_inc(self.x_in, 1)

            def dve_hid(self, dve, e):
                dve.wait_ge(self.silued, after(e))
                dve.wait_ge(self.used[1], after(NS * e + NS - 1))
                dve.wait_ge(self.used[2], after(NS * e - 1))
                dve.tensor_tensor(self.hidT.rearrange("p (b c) t -> p b (c t)", b=2), self.silu.rearrange("p (b c) t -> p b (c t)", b=2),
                                  score_ps[:, :, 0:4 * CAP], ALU.mult).then_inc(self.hidden, 1)

            def dve_yT(self, dve, e):
                dve.wait_ge(self.used[2], after(NS * e + NS - 1))
                dve.wait_ge(self.y_turned, after(e - 1))
                dve.tensor_copy(self.yT.rearrange("p (b c) t -> p b (c t)", b=2), pT_ps[:, :, 0:4 * CAP]).then_inc(self.yT_in, 1)

            def dve(self, l):
                def f(dve):
                    e0, e1 = NE * l, NE * l + NE
                    self.dve_x(dve, l, e0)
                    self.dve_x(dve, l, e0 + 1)
                    self.dve_hid(dve, e0)
                    with dve.Fori(e0 + 1, e1 - 1) as e:
                        self.dve_x(dve, l, e + 1)
                        self.dve_yT(dve, e - 1)
                        self.dve_hid(dve, e)
                    self.dve_yT(dve, e1 - 2)
                    self.dve_hid(dve, e1 - 1)
                    self.dve_yT(dve, e1 - 1)
                return f

            def gather(self, pool, l, e, first=False):
                if not first:
                    pool.wait_ge(self.gathered, 16 * e)
                pool.wait_ge(self.x_turned, after(e - 1))
                pool.tensor_copy(self.gather_idx[:CAP, :], idxT[:CAP, bass.ds(e, 1)]).then_inc(self.listed, 1)
                pool.wait_ge(self.listed, e + 1)
                settle(pool)
                pool.indirect_dma_start(self.xe[:CAP, :], None, xn_dram[l],
                                        bass.IndirectOffsetOnAxis(self.gather_idx[:CAP, :], 0)).then_inc(self.gathered, 16)

            def scatter(self, pool, l, e):
                pool.wait_ge(self.y_out, after(e))
                pool.tensor_copy(self.scatter_idx[:CAP, :], idxT[:CAP, bass.ds(e, 1)]).then_inc(self.relisted, 1)
                pool.wait_ge(self.relisted, e + 1)
                settle(pool)
                pool.indirect_dma_start(acc_dram[l], bass.IndirectOffsetOnAxis(self.scatter_idx[:CAP, :], 0),
                                        self.y[:CAP, :], None, compute_op=ALU.add).then_inc(self.scattered, 16)

            def pool(self, l):
                def f(pool):
                    e0, e1 = NE * l, NE * l + NE
                    self.gather(pool, l, e0, l == 0)
                    self.gather(pool, l, e0 + 1)
                    self.gather(pool, l, e0 + 2)
                    with pool.Fori(e0 + 2, e1 - 1) as e:
                        self.gather(pool, l, e + 1)
                        self.scatter(pool, l, e - 2)
                    for e in range(e1 - 3, e1):
                        self.scatter(pool, l, e)
                    pool.wait_ge(self.scattered, 16 * e1)
                return f

        CONSTS = 48
        norms = {n: Norm(n, k) for k, n in enumerate(("mix0", "ffn0", "mix1", "ffn1", "final"))}
        mix_a, mix_b, mix_c = MixerA(), MixerB(), MixerC()
        outs = [OutProject(l) for l in range(2)]
        routes = [Route(l) for l in range(2)]
        experts = Experts()
        final = norms["final"]
        fc = Carve(8 * D)
        final_gain = fc(D)
        y_sb = fc(NT, D)
        final_in, final_y, final_stored = sem("final_gain_in"), sem("final_y"), sem("final_stored")

        def run(eng, steps):
            for n in phases:
                for f in steps.get(n, ()):
                    f(eng)
                if n != "final":
                    end_phase(eng, n)

        block = es.enter_context(nc.Block())

        @block.sync
        def _(sp):
            for s in seeded:
                sp.sem_inc(s, 2)

            def load_x(sp):
                sp.dma_start(x[:], x_in.rearrange("(t p) n -> p t n", p=P)).then_inc(x_loaded, 16)
                sp.dma_start(ident[:], ident_in).then_inc(consts_in, 16)
                sp.dma_start(gcol[:], gains).then_inc(consts_in, 16)
                sp.dma_start(router_sb[:], router).then_inc(consts_in, 16)
                mix_c.windows(sp)

            def reload_x(l, name):
                def f(sp):
                    sp.dma_start(x[:], acc_dram[l].rearrange("(t p) n -> p t n", p=P)).then_inc(x_loaded, 16)
                return f

            def store_rows(l):
                def f(sp):
                    nm = norms[f"ffn{l}"]
                    sp.dma_start(acc_dram[l].rearrange("(t p) n -> p t n", p=P), x[:]).then_inc(rows_stored, 16)
                    for t in range(NT):
                        sp.wait_ge(norm_scaled, nm.t0 + t + 1)
                        sp.dma_start(xn_dram[l][t * P:(t + 1) * P], nm.xn[:, t]).then_inc(rows_stored, 16)
                    sp.wait_ge(rows_stored, 16 * (NT + 1) * (l + 1))
                return f

            def a_stores_landed(sp):
                mix_a.stored(sp, sum(mix_a.tiles(g) for g in range(GROUPS)))

            def store_y(sp):
                for t in range(NT):
                    sp.wait_ge(final_y, t + 1)
                    sp.dma_start(y_out[t * P:(t + 1) * P], y_sb[:, t]).then_inc(final_stored, 16)
                sp.wait_ge(final_stored, 16 * NT)

            run(sp, {"mix0": [load_x], "a": [mix_a.sp, a_stores_landed], "join": [mix_a.join_sp], "b": [mix_b.sp], "out0": [outs[0].sp],
                     "ffn0": [store_rows(0)], "route0": [experts.sp_first(0)], "moe0": [experts.sp(0)],
                     "mix1": [reload_x(0, "mix1")], "c": [mix_c.sp], "out1": [outs[1].sp],
                     "ffn1": [store_rows(1)], "route1": [experts.sp_first(1)], "moe1": [experts.sp(1)],
                     "final": [reload_x(1, "final"),
                               lambda sp: sp.dma_start(final_gain, final_g.to_broadcast([P, D])).then_inc(final_in, 16),
                               store_y]})

        @block.tensor
        def _(pe):
            run(pe, {"mix0": [norms["mix0"].pe], "a": [mix_a.pe], "join": [mix_a.join_pe], "b": [mix_b.pe], "out0": [outs[0].pe],
                     "ffn0": [norms["ffn0"].pe], "route0": [routes[0].pe], "moe0": [experts.pe(0)],
                     "mix1": [norms["mix1"].pe], "c": [mix_c.pe], "out1": [outs[1].pe],
                     "ffn1": [norms["ffn1"].pe], "route1": [routes[1].pe], "moe1": [experts.pe(1)]})

        @block.scalar
        def _(act):
            run(act, {"mix0": [norms["mix0"].act], "a": [mix_a.act], "join": [mix_a.join_act], "b": [mix_b.act],
                      "ffn0": [norms["ffn0"].act], "route0": [routes[0].act], "moe0": [experts.act(0)],
                      "mix1": [norms["mix1"].act], "c": [mix_c.act],
                      "ffn1": [norms["ffn1"].act], "route1": [routes[1].act], "moe1": [experts.act(1)],
                      "final": [final.act]})

        @block.vector
        def _(dve):
            def final_dve(dve):
                final.dve_stats(dve)
                dve.wait_ge(final_in, 16)
                for t in range(NT):
                    dve.wait_ge(norm_scaled, final.t0 + t + 1)
                    dve.tensor_tensor(y_sb[:, t], final.xn[:, t], final_gain, ALU.mult).then_inc(final_y, 1)

            run(dve, {"mix0": [norms["mix0"].dve], "a": [mix_a.dve], "join": [mix_a.join_dve], "b": [mix_b.dve], "out0": [outs[0].dve],
                      "ffn0": [norms["ffn0"].dve], "route0": [routes[0].dve], "moe0": [experts.dve(0)],
                      "mix1": [norms["mix1"].dve], "c": [mix_c.dve], "out1": [outs[1].dve],
                      "ffn1": [norms["ffn1"].dve], "route1": [routes[1].dve], "moe1": [experts.dve(1)],
                      "final": [final_dve]})

        @block.gpsimd
        def _(pool):
            run(pool, {"moe0": [experts.pool(0)], "c": [mix_c.pool], "moe1": [experts.pool(1)]})


def shape_constants():
    import numpy as np

    def bucket(rel):
        n = np.abs(rel)
        large = 8 + (np.log(np.maximum(n, 1) / 8) / np.log(1024 / 8) * 8).astype(np.int32)
        return np.where(rel > 0, 16, 0) + np.where(n < 8, n, np.minimum(large, 15))

    onehot = np.zeros((33, 1024), np.float32)
    for at, n, zero, kind in ((0, 512, 255, 0), (512, 256, 127, 1), (768, 256, 127, 2)):
        d = np.arange(n) - zero
        if kind == 0:
            ok, rel = np.abs(d) <= 64, d
        elif kind == 1:
            ok, rel = np.abs(d) <= 64, 4 * d
        else:
            ok, rel = (d % 4 == 0) & (np.abs(d) <= 256), 4 * d
        b = bucket(rel)
        for i in range(n):
            onehot[b[i] if ok[i] else 32, at + i] = 1.0

    col_mask = np.zeros((128, 7, 16), np.float32)
    c, kc = np.arange(16)[:, None], np.arange(16)[None]
    for first, j, deltas in ((0, 0, (0, 1)), (2, 1, (-1, 0, 1)), (5, 3, (-1, 0))):
        qcol = 16 * j + c
        start = np.clip(qcol - 8, 0, 48)
        for n, d in enumerate(deltas):
            key = 16 * (j + d) + kc
            m = np.where((key >= start) & (key < start + 16), 0.0, MASKED).astype(np.float32)
            col_mask[:, first + n] = np.tile(m, (8, 1))

    inv = 1.0 / (10000.0 ** (np.arange(0, 32, 2, dtype=np.float32) / 32))
    pos = np.concatenate([np.arange(PROMPT), np.arange(SAMPLE)]).astype(np.float32)
    ang = pos[:, None] * inv[None].astype(np.float32)
    cos, sin = np.cos(ang).astype(np.float32), np.sin(ang).astype(np.float32)
    scale = np.float32(96 ** -0.5)
    q_table = np.ascontiguousarray(np.concatenate([np.ones((64, TOK), np.float32), cos.T, cos.T, -sin.T, sin.T]) * scale).astype(np.float32)
    rope = np.ascontiguousarray(np.stack([cos, sin], 1).reshape(NT, P, 2, 16).transpose(1, 0, 2, 3))
    return onehot, col_mask, q_table, rope


def kernel(x_prompt, x_sample, ln_mix_g, w_in_even, g_qa, w_qb, g_kva, w_kvb, t5_table, w_out_even,
           w_in_odd, rpb, w_out_odd, ln_ffn_g, router, w_gate, w_up, w_down, final_g):
    import numpy as np
    import concourse.bacc as bacc
    from concourse.bass_utils import run_bass_kernel_spmd

    a = np.asarray

    def rows(w):
        return a(w).reshape(-1, P, w.shape[-1]).transpose(1, 0, 2)

    def column(g):
        return a(g).reshape(-1, P).T

    onehot, col_mask, q_table, rope = shape_constants()
    wa = a(w_in_even)[0][:, :A_IN].reshape(D, 3, GROUPS, AH * HD)
    wb = a(w_in_even)[0][:, A_IN:]
    qb = a(w_qb)[0].reshape(QR, 2 * B_PAIRS, 96)
    qb = np.concatenate([qb, qb[:, :, 80:96], qb[:, :, 64:80]], axis=2).reshape(3, P, B_PAIRS, 256)
    kvb = a(w_kvb)[0].reshape(2, P, B_PAIRS, 2, 2, HD).transpose(2, 1, 0, 4, 3, 5).reshape(B_PAIRS, P, 2, 256)
    wc = a(w_in_odd)[0].reshape(DC, P, 3, C_PAIRS, P).transpose(3, 1, 0, 2, 4).reshape(C_PAIRS, P, DC, 384)
    rpb_wide = np.zeros((2 * C_PAIRS, DROWS, 64), a(rpb).dtype)
    rpb_wide[:, :, 16:47] = a(rpb)[0]
    arrays = {
        "x_in": np.concatenate([a(x_prompt).reshape(-1, D), a(x_sample).reshape(-1, D)]),
        "gains": np.concatenate([column(ln_mix_g[0]), column(ln_ffn_g[0]), column(ln_mix_g[1]), column(ln_ffn_g[1]),
                                 column(g_qa[0]), column(g_kva[0])], axis=1),
        "w_a": np.stack([rows(wa[:, :, g].reshape(D, 768)) for g in range(GROUPS)]),
        "w_b": rows(wb),
        "w_qb_pairs": qb.transpose(2, 1, 0, 3),
        "w_kvb_pairs": kvb,
        "w_out": np.stack([rows(a(w_out_even)[0]), rows(a(w_out_odd)[0])]),
        "w_c": wc,
        "t5": a(t5_table),
        "onehot": onehot,
        "rpb_wide": rpb_wide,
        "router_cols": np.stack([rows(a(router)[0]), rows(a(router)[1])], axis=1),
        "w_gate": a(w_gate), "w_up": a(w_up), "w_down": a(w_down),
        "final_row": a(final_g).reshape(1, D),
        "ident_in": np.eye(P, dtype=np.float32),
        "col_mask": col_mask, "q_table": q_table, "rope_in": rope,
    }
    arrays = {k: np.ascontiguousarray(v) for k, v in arrays.items()}
    nc = bacc.Bacc("TRN2", target_bir_lowering=False, num_devices=1)
    aps = [nc.dram_tensor(k, v.shape, mybir.dt.from_np(v.dtype), kind="ExternalInput").ap() for k, v in arrays.items()]
    y = nc.dram_tensor("y_out", (TOK, D), F32, kind="ExternalOutput").ap()
    program(nc, *aps, y)
    got = run_bass_kernel_spmd(nc, [arrays], core_ids=[0]).results[0]["y_out"]
    return got[:PROMPT].reshape(1, PROMPT, D), got[PROMPT:].reshape(1, SAMPLE, D)
```

```python
from contextlib import ExitStack

import concourse.bass as bass
from concourse import mybir

F32 = mybir.dt.float32
F32R = mybir.dt.float32r
U32 = mybir.dt.uint32
ALU = mybir.AluOpType
ACT = mybir.ActivationFunctionType
AX = mybir.AxisListType

P = 128
D = 1024
DC = D // P
PROMPT, SAMPLE = 512, 256
TOK = PROMPT + SAMPLE
NT = TOK // P
HALF = TOK // 2
HD = 64
EPS = 1e-6
MASKED = -1e30
GROUPS = 3
AH = 4
A_IN = 3 * GROUPS * AH * HD
QR, KVR, ROPE = 384, 256, 32
B_IN = QR + KVR + ROPE
B_PAIRS = 6
C_PAIRS = 8
GRID = 64
CB = 16
NB = GRID // CB
C_ROWS, S_ROWS = PROMPT // GRID, SAMPLE // GRID
WIN = 3 * CB
DROWS = 15
NE = 16
FF = 1024
CAP_P, CAP_S = 2 * PROMPT // NE, 2 * SAMPLE // NE
CAP = CAP_P + CAP_S
OROW = AH * (HD + 2)
S_AT, S_END = 32, 32 + NE
LOW = -3.0e38
ARENA = 33920
C_PARTS_AT = 11392
SL = 2
NS = DC // SL
RAW = 3 * NS
PARTS = 3


def after(n):
    return n + 3


class Unit:

    def __init__(self, nq, heads, kt, tiles, first_key, tile, last):
        self.nq, self.heads, self.kt, self.tiles = nq, heads, kt, tiles
        self.nk = kt * len(tiles)
        self.first_key = first_key
        self.tile = tile
        self.last = last

    def cols(self, h):
        return slice(h * self.nk, (h + 1) * self.nk)


def near_tiles(t, n):
    return list(range(max(t - 1, 0), min(t + 2, n)))


def units_near(nq, heads_pairs, t, tile, n, base):
    near = near_tiles(t, n)
    groups = [[h, h + 1] for h in heads_pairs] if len(near) < 3 else [[h + d] for h in heads_pairs for d in (0, 1)]
    return [Unit(nq, g, nq, [base + m for m in near], t, tile, g is groups[-1]) for g in groups]


def units_a(g):
    if g == 0:
        us = [u for t in range(4) for u in units_near(P, (0, 2), t, t, 4, 0)]
        return us + [u for t in range(2) for u in units_near(P, (0, 2), t, 4 + t, 2, 4)]
    us = [Unit(P, [0, 1, 2, 3], P, [t], t, t, True) for t in range(4)]
    return us + [Unit(HD, [0, 1, 2, 3], HD, [4 + t], t, 4 + t, True) for t in range(4)]


def units_b():
    us = [Unit(P, [h], P, [0, 1, 2, 3], 0, t, h == 1) for t in range(4) for h in (0, 1)]
    return us + [Unit(P, [0, 1], P, [4, 5], 0, t, True) for t in (4, 5)]


def units_c():
    us = [u for j in range(NB) for u in units_near(P, (0,), j, j, NB, 0)]
    return us + [u for j in range(NB) for u in units_near_sample(j)]


def units_near_sample(j):
    near = near_tiles(j, NB)
    return [Unit(CB * S_ROWS, [0, 1], CB * S_ROWS, [NB + m for m in near], j, NB + j, True)]


C_BIAS0 = [0, 2, 2, 5]


def tokens_a(ap, g, t):
    if g == 0:
        return ap[:, t * P:(t + 1) * P]
    part = ap[:, 0:PROMPT] if t < 4 else ap[:, PROMPT:TOK]
    t %= 4
    return part.rearrange("p (l r) -> p l r", r=4)[:, :, t]


def tokens_c(ap, t):
    part = ap[:, 0:PROMPT] if t < NB else ap[:, PROMPT:TOK]
    t %= NB
    return part.rearrange("p (r w) -> p r w", w=GRID)[:, :, t * CB:(t + 1) * CB]


def run_c(ap, t, n=1):
    if t < NB:
        return ap[:, t * P:(t + n) * P]
    w = CB * S_ROWS
    return ap[:, PROMPT + (t - NB) * w:PROMPT + (t - NB + n) * w]


def program(nc, x_in, gains, w_a, w_b, w_qb, w_kvb, w_out, w_c, t5, onehot, rpb, router, w_gate, w_up, w_down,
            final_g, ident_in, col_mask, q_table, rope_in, y_out):
    es = ExitStack()
    with es:
        def sb(name, shape, dt=F32):
            return es.enter_context(nc.sbuf_tensor(name, shape, dt))

        def ps(name, shape):
            return es.enter_context(nc.psum_tensor(name, shape, F32))

        def sem(name):
            return es.enter_context(nc.semaphore(name))

        def dram(name, shape):
            return nc.dram_tensor(name, shape, F32, kind="Internal").ap()

        f_dram = dram("t5_by_distance", (12, 1024))
        shifted_dram = dram("t5_shifted", (CB, 12, 1024 - CB))
        window_dram = dram("rpb_windows", (CB, 2 * C_PAIRS, DROWS, WIN))
        oa_dram = dram("mixer_a_groups", (GROUPS, TOK, OROW))
        xn_dram = [dram(f"normed_rows{l}", (TOK, D)) for l in range(2)]
        acc_dram = [dram(f"residual_rows{l}", (TOK, D)) for l in range(2)]

        with ExitStack() as shared:
            def part(name, *shape):
                return shared.enter_context(nc.sbuf_tensor(name, [P, *shape], F32R))

            assert PARTS * SL * FF == NT * D == DC * TOK
            w_hi = part("w_hi", PARTS, SL, FF)
            x_hi, x_lo, h_hi, h_lo = (part(k, DC, CAP) for k in ("x_hi", "x_lo", "h_hi", "h_lo"))
            shared.enter_context(nc.sbuf_tensor("rest_of_hT", [P, DC * TOK - 4 * DC * CAP], F32))
            w_lo = part("w_lo", PARTS, SL, FF)
        with ExitStack() as shared:
            shared.enter_context(nc.sbuf_tensor("below_hT", [P, NT * D], F32))
            n_hi = part("n_hi", DC, TOK)
            shared.enter_context(nc.sbuf_tensor("below_n_lo", [P, DC * TOK + C_PARTS_AT], F32))
            n_lo = part("n_lo", DC, TOK)
            qk_hi, qk_lo, v_hi, v_lo = (part(f"c_{k}", DC, 2 * P) for k in ("qk_hi", "qk_lo", "v_hi", "v_lo"))
            assert C_PARTS_AT + DC * TOK + 4 * DC * 2 * P <= ARENA - DC * D
        with ExitStack() as shared:
            shared.enter_context(nc.sbuf_tensor("below_arena", [P, NT * D + 2 * DC * TOK], F32))
            wo_hi = part("wo_hi", DC, D)
            shared.enter_context(nc.sbuf_tensor("below_wo_lo", [P, C_PARTS_AT + DC * TOK - DC * D], F32))
            wo_lo = part("wo_lo", DC, D)
            assert C_PARTS_AT + DC * TOK + DC * D <= ARENA - DC * D
        x = sb("x", [P, NT, D])
        hT = sb("hT", [P, DC, TOK])
        aT = sb("aT", [P, DC, TOK])
        arena = sb("arena", [P, ARENA])
        ident = sb("ident", [P, P])
        gcol = sb("gcol", [P, 37])
        g_of = {"mix0": gcol[:, 0:8], "ffn0": gcol[:, 8:16], "mix1": gcol[:, 16:24], "ffn1": gcol[:, 24:32]}
        gq, gkv = gcol[:, 32:35], gcol[:, 35:37]
        router_sb = sb("router_sb", [P, 2, DC, NE])
        smax = sb("smax", [P, 16, AH])
        nmax = sb("nmax", [P, 16, AH])
        den = sb("den", [P, 16, AH])
        rden = sb("rden", [P, 16, AH])
        stat = sb("stat", [P, 5, NT])
        rstd = sb("rstd", [P, 5, NT])
        bstat = sb("bstat", [P, 2, NT])
        brstd = sb("brstd", [P, 2, NT])

        class Carve:

            def __init__(self, at=0):
                self.at = at

            def __call__(self, *shape):
                n = 1
                for s in shape:
                    n *= s
                a = arena[:, self.at:self.at + n]
                self.at += n
                assert self.at <= ARENA, self.at
                if len(shape) == 1:
                    return a
                names = " ".join(f"d{i}" for i in range(len(shape)))
                return a.rearrange(f"p ({names}) -> p {names}", **{f"d{i}": s for i, s in enumerate(shape)})

        proj_ps = ps("proj_ps", [P, 2, 512])
        score_ps = ps("score_ps", [P, 2, 512])
        pT_ps = ps("pT_ps", [P, 2, 512])
        o_ps = ps("o_ps", [P, 2, 512])

        seeded = []

        def slots(name):
            s = sem(name)
            seeded.append(s)
            return s

        phases = ["mix0", "a", "join", "b", "out0", "ffn0", "route0", "moe0", "mix1", "c", "out1", "ffn1", "route1", "moe1", "final"]
        ended = sem("ended")

        def end_phase(eng, name):
            eng.drain().then_inc(ended, 1)
            eng.wait_ge(ended, 5 * (phases.index(name) + 1))

        settled = sem("settled")

        def settle(eng):
            eng.sem_inc(settled, 1)

        consts_in = sem("consts_in")

        class Norm:
            def __init__(self, name, k):
                self.name, self.k = name, k
                c = Carve(ARENA - 8 * D)
                self.xn = c(NT, D)
                self.junk = Carve(DC * D)(D) if name.startswith("ffn") else c(D)
                if name == "mix1":
                    self.scaled_rows = c(2, 512)
                    self.hi_made = sem("norm_hi_made")
                self.reloads = ("mix0", "mix1", "final").index(name) + 1 if name in ("mix0", "mix1", "final") else 0
                self.t0, self.n0 = NT * k, 2 * NT * k

            def act_squares(self, act):
                for t in range(NT):
                    if self.reloads and t % 2 == 0:
                        act.wait_ge(x_loaded[t // 2], 16 * self.reloads)
                    if not self.reloads:
                        act.wait_ge(out_added, after(2 * NT * (self.k // 2) + NT + t))
                    if t:
                        act.wait_ge(norm_squares, self.t0 + t)
                    act.activation(self.junk, x[:, t], ACT.Square, accum_out=stat[:, self.k, t:t + 1]).then_inc(norm_squares, 1)

            def act(self, act):
                if self.reloads:
                    self.act_squares(act)
                act.wait_ge(norm_mean, self.k + 1)
                act.activation(rstd[:, self.k], rstd[:, self.k], ACT.Sqrt).then_inc(norm_root, 1)
                act.wait_ge(norm_rstd, self.k + 1)
                for t in range(NT):
                    act.activation(self.xn[:, t], x[:, t], ACT.Copy, scale=rstd[:, self.k, t:t + 1]).then_inc(norm_scaled, 1)

            def dve_stats(self, dve):
                dve.wait_ge(norm_squares, self.t0 + NT)
                dve.tensor_scalar(rstd[:, self.k], stat[:, self.k], 1.0 / D, EPS, ALU.mult, ALU.add).then_inc(norm_mean, 1)
                dve.wait_ge(norm_root, self.k + 1)
                dve.reciprocal(rstd[:, self.k], rstd[:, self.k]).then_inc(norm_rstd, 1)

            def pe(self, pe, beside=None):
                pe.wait_ge(consts_in, CONSTS)
                for t in range(NT):
                    pe.wait_ge(norm_scaled, self.t0 + t + 1)
                    for half in range(2):
                        n = self.n0 + 2 * t + half
                        pe.wait_ge(norm_evac, after(n - 2))
                        for c in range(4):
                            k = 4 * half + c
                            last = pe.transpose(proj_ps[:, half, c * P:(c + 1) * P], self.xn[:, t, k * P:(k + 1) * P], ident[:])
                        last.then_inc(norm_turned, 1)
                    if beside and t:
                        pe.wait_ge(norm_evac, after(self.n0 + 2 * t - 1))
                        beside(pe, t - 1)
                if beside:
                    pe.wait_ge(norm_evac, after(self.n0 + 2 * NT - 1))
                    beside(pe, NT - 1)

            def dve(self, dve):
                self.dve_stats(dve)
                g = g_of[self.name]
                dve.wait_ge(consts_in, CONSTS)
                for n in range(2 * NT):
                    t, half = n // 2, n % 2
                    dve.wait_ge(norm_turned, after(self.n0 + n))
                    gg = g[:, 4 * half:4 * half + 4]
                    src = proj_ps[:, half].rearrange("p (c t) -> p c t", c=4)
                    if self.name == "mix1":
                        slot = self.scaled_rows[:, n % 2].rearrange("p (c t) -> p c t", c=4)
                        dve.tensor_tensor(slot, src, gg.unsqueeze(2).to_broadcast([P, 4, P]), ALU.mult).then_inc(norm_evac, 1)
                        dve.wait_ge(self.hi_made, n + 1)
                        for (hi, lo), rows in zip(self.places(t, half), self.rows(n)):
                            last = dve.tensor_tensor(lo, rows, hi.bitcast(F32), ALU.subtract)
                        continue
                    dve.tensor_tensor(hT[:, 4 * half:4 * half + 4, t * P:(t + 1) * P], src,
                                      gg.unsqueeze(2).to_broadcast([P, 4, P]), ALU.mult).then_inc(norm_evac, 1)

            def places(self, t, half):
                base, rows, row0 = (0, C_ROWS, 2 * t) if t < 4 else (PROMPT, S_ROWS, 2 * (t - 4))
                return [[a[:, 4 * half:4 * half + 4, base:base + NB * rows * CB].rearrange("p k (b r c) -> p k b r c", b=NB, r=rows)[:, :, :, row0 + r]
                         for a in (n_hi, n_lo)] for r in range(P // GRID)]

            def rows(self, n):
                slot = self.scaled_rows[:, n % 2].rearrange("p (c r b w) -> p c r b w", c=4, r=P // GRID, b=NB)
                return [slot[:, :, r] for r in range(P // GRID)]

            def act_hi(self, act, beside):
                for n in range(2 * NT):
                    if n in beside:
                        beside[n](act)
                    act.wait_ge(norm_evac, after(self.n0 + n))
                    for (hi, lo), rows in zip(self.places(n // 2, n % 2), self.rows(n)):
                        last = act.activation(hi, rows, ACT.Copy)
                    last.then_inc(self.hi_made, 1)

        x_loaded = [sem(f"x_loaded{i}") for i in range(NT // 2)]
        norm_squares = sem("norm_squares")
        norm_mean = sem("norm_mean")
        norm_root = sem("norm_root")
        norm_rstd = sem("norm_rstd")
        norm_scaled = sem("norm_scaled")
        norm_turned = slots("norm_turned")
        norm_evac = slots("norm_evac")
        rows_stored = sem("rows_stored")

        class Attention:

            def __init__(self, name, carve, bias):
                self.name, self.bias = name, bias
                self.probs = carve(2, 512)
                self.pT = carve(2, 512)
                self.scored = slots(f"{name}_scored")
                self.maxed = slots(f"{name}_maxed")
                self.negated = slots(f"{name}_negated")
                self.exped = slots(f"{name}_exped")
                self.turned = slots(f"{name}_turned_p")
                self.pT_in = slots(f"{name}_pT_in")
                self.summed = slots(f"{name}_summed")
                self.inverted = slots(f"{name}_inverted")
                self.o_out = slots(f"{name}_o_out")
                self.o_turned = slots(f"{name}_o_turned")
                self.o_in = slots(f"{name}_o_in")

            def pe(self, pe, units, u0, t0, q, k, v, o_sb, beside=None):
                n, tile = len(units), 0
                for j in range(n + 4):
                    if j < n:
                        u = units[j]
                        pe.wait_ge(self.maxed if self.bias else self.exped, after(u0 + j - 2))
                        for i, h in enumerate(u.heads):
                            last = pe.matmul(score_ps[:u.nq, j % 2, u.cols(i)], q(u, h), k(u, h), start=True, stop=True)
                        last.then_inc(self.scored, 1)
                    elif beside:
                        beside(j - n)
                    if 2 <= j <= n + 1:
                        u, b = units[j - 2], j % 2
                        pe.wait_ge(self.exped, after(u0 + j - 2))
                        pe.wait_ge(self.pT_in, after(u0 + j - 4))
                        if u.kt < P:
                            settle(pe)
                        for i in range(len(u.heads) * len(u.tiles)):
                            last = pe.transpose(pT_ps[:u.kt, b, i * u.nq:(i + 1) * u.nq],
                                                self.probs[:u.nq, b, i * u.kt:(i + 1) * u.kt], ident[:u.nq, :u.nq])
                        last.then_inc(self.turned, 1)
                    if 3 <= j <= n + 2:
                        u, b = units[j - 3], (j - 3) % 2
                        pe.wait_ge(self.pT_in, after(u0 + j - 3))
                        pe.wait_ge(self.o_out, after(u0 + j - 4))
                        if u.kt < P:
                            settle(pe)
                        for i, h in enumerate(u.heads):
                            for m, t in enumerate(u.tiles):
                                at = (i * len(u.tiles) + m) * u.nq
                                last = pe.matmul(o_ps[:u.nq, 0, i * HD:(i + 1) * HD],
                                                 self.pT[:u.kt, b, at:at + u.nq], v(u, h, t),
                                                 start=(m == 0), stop=(m == len(u.tiles) - 1))
                        last.then_inc(self.summed, 1)
                    if o_sb is not None and j >= 4 and units[j - 4].last:
                        u, b = units[j - 4], tile % 2
                        pe.wait_ge(self.o_out, after(u0 + j - 4))
                        pe.wait_ge(self.o_in, after(t0 + tile - 1))
                        if u.nq < P:
                            settle(pe)
                        pe.transpose(o_ps[:, 1, :u.nq], o_sb[:u.nq, b], ident[:u.nq, :u.nq]).then_inc(self.o_turned, 1)
                        tile += 1

            def dve(self, dve, units, u0, t0, bias, out, turned_out, beside=None):
                n, tile, done = len(units), 0, 0
                for j in range(n + 4):
                    if j < n:
                        u, b = units[j], j % 2
                        dve.wait_ge(self.scored, after(u0 + j))
                        if self.bias:
                            dve.wait_ge(self.turned, after(u0 + j - 2))
                            settle(dve)
                            for i, h in enumerate(u.heads):
                                bb = bias(u, h)
                                shape = "p (b r c) -> p b r c" if len(bb.shape) == 4 else None
                                s, o = score_ps[:u.nq, b, u.cols(i)], self.probs[:u.nq, b, u.cols(i)]
                                if shape:
                                    dims = dict(b=bb.shape[1], r=bb.shape[2])
                                    s, o = s.rearrange(shape, **dims), o.rearrange(shape, **dims)
                                elif len(bb.shape) == 3:
                                    s, o = (y.rearrange("p (b c) -> p b c", b=bb.shape[1]) for y in (s, o))
                                last = dve.tensor_tensor_reduce(o, s, bb, 1.0, LOW, ALU.add, ALU.max, smax[:u.nq, j, i:i + 1])
                            last.then_inc(self.maxed, 1)
                            dve.wait_ge(self.maxed, after(u0 + j))
                            dve.tensor_scalar(nmax[:u.nq, j, :len(u.heads)], smax[:u.nq, j, :len(u.heads)], -1.0, None,
                                              ALU.mult).then_inc(self.negated, 1)
                        else:
                            dve.tensor_reduce(nmax[:u.nq, j, :len(u.heads)],
                                              score_ps[:u.nq, b, :u.nk * len(u.heads)].rearrange("p (h k) -> p h k", k=u.nk),
                                              AX.X, ALU.max, negate=True).then_inc(self.negated, 1)
                    if 3 <= j <= n + 2:
                        u = units[j - 3]
                        dve.wait_ge(self.summed, after(u0 + j - 3))
                        out(dve, u, j - 3, u0, t0, done, o_ps[:u.nq, 0, :len(u.heads) * HD])
                        done += u.last
                    if turned_out is not None and j >= 4 and units[j - 4].last:
                        u = units[j - 4]
                        dve.wait_ge(self.o_turned, after(t0 + tile))
                        dve.tensor_copy(turned_out(u), o_ps[:, 1, :u.nq] if len(turned_out(u).shape) == 2 else
                                        o_ps[:, 1, :u.nq].rearrange("p (r c) -> p r c", c=CB)).then_inc(self.o_in, 1)
                        tile += 1
                    if beside and j >= n:
                        beside(j - n)

            def normalised(self, o_sb):
                def out(dve, u, j, u0, t0, tile, o):
                    k = len(u.heads)
                    dve.reciprocal(rden[:u.nq, j, :k], den[:u.nq, j, :k]).then_inc(self.inverted, 1)
                    dve.wait_ge(self.o_turned, after(t0 + tile - 2))
                    dve.wait_ge(self.inverted, after(u0 + j))
                    for i, h in enumerate(u.heads):
                        last = dve.tensor_scalar(o_sb[:u.nq, tile % 2, h * HD:(h + 1) * HD], o[:, i * HD:(i + 1) * HD],
                                                 rden[:u.nq, j, i:i + 1], None, ALU.mult)
                    last.then_inc(self.o_out, 1)
                return out

            def act(self, act, units, u0, beside=None, middle=None):
                n = len(units)
                for j in range(n + 2):
                    if j >= 2:
                        u, b = units[j - 2], j % 2
                        act.wait_ge(self.turned, after(u0 + j - 2))
                        act.wait_ge(self.summed, after(u0 + j - 4))
                        w = len(u.heads) * len(u.tiles) * u.nq
                        act.activation(self.pT[:u.kt, b, :w], pT_ps[:u.kt, b, :w], ACT.Copy).then_inc(self.pT_in, 1)
                    if j < n:
                        u, b = units[j], j % 2
                        act.wait_ge(self.negated, after(u0 + j))
                        if not self.bias:
                            act.wait_ge(self.turned, after(u0 + j - 2))
                        src = self.probs if self.bias else score_ps
                        for i in range(len(u.heads)):
                            last = act.activation(self.probs[:u.nq, b, u.cols(i)], src[:u.nq, b, u.cols(i)], ACT.Exp,
                                                  bias=nmax[:u.nq, j, i:i + 1], accum_out=den[:u.nq, j, i:i + 1])
                        last.then_inc(self.exped, 1)
                    elif beside:
                        beside(j - n)
                    if middle and j == n // 2:
                        middle()

        class Project:

            def __init__(self, name):
                self.ready = slots(f"{name}_ready")
                self.act_out = slots(f"{name}_act_out")
                self.dve_out = slots(f"{name}_dve_out")

            def pe_one(self, pe, blocks, h0, n):
                pe.wait_ge(self.dve_out if n % 2 else self.act_out, after(h0 + n // 2 - 1))
                blocks[n](pe, proj_ps[:, n % 2]).then_inc(self.ready, 1)

            def pe(self, pe, blocks, h0, first=0):
                for n in range(first, len(blocks)):
                    self.pe_one(pe, blocks, h0, n)

            def out_one(self, eng, copies, h0, n):
                eng.wait_ge(self.ready, after(2 * h0 + n))
                copies[n](eng, proj_ps[:, n % 2]).then_inc(self.dve_out if n % 2 else self.act_out, 1)

            def out(self, eng, odd, copies, h0, first=0):
                for n in range(first + odd, len(copies), 2):
                    self.out_one(eng, copies, h0, n)

            def act_beside(self, act, copies, h0):
                return lambda d: self.out_one(act, copies, h0, 2 * d)

            def dve_beside(self, dve, copies, h0):
                return lambda d: self.out_one(dve, copies, h0, d) if d % 2 else None

            def all_out(self, eng, half_blocks):
                eng.wait_ge(self.act_out, after(half_blocks - 1))
                eng.wait_ge(self.dve_out, after(half_blocks - 1))

        def product(out, lhs, rhs, n):
            def block(pe, bank):
                for c in range(n):
                    last = pe.matmul(out(bank), lhs(c), rhs(c), start=(c == 0), stop=(c == n - 1))
                return last
            return block

        def product3(out, lhs, rhs, n):
            def block(pe, bank):
                for c in range(n):
                    (a_hi, a_lo), (b_hi, b_lo) = lhs(c), rhs(c)
                    for k, (a, b) in enumerate(((a_hi, b_hi), (a_hi, b_lo), (a_lo, b_hi))):
                        last = pe.matmul(out(bank), a, b, start=(c == 0 and k == 0), stop=(c == n - 1 and k == 2))
                return last
            return block

        def wide(*blocks):
            def block(pe, bank):
                for b in blocks:
                    last = b(pe, bank)
                return last
            return block

        def copy_to(dst, src, scale=None):
            def copy(eng, bank):
                if eng.engine == mybir.EngineType.Activation:
                    return eng.activation(dst, src(bank), ACT.Copy, scale=1.0 if scale is None else scale)
                if scale is None:
                    return eng.tensor_copy(dst, src(bank))
                return eng.tensor_scalar(dst, src(bank), scale, None, ALU.mult)
            return copy

        def split_heads(q, scale):
            def copy(eng, bank):
                for h in range(2):
                    r = slice(h * HD, (h + 1) * HD)
                    last = copy_to(q(h)[r], lambda bank: bank[r, 0:HALF], scale)(eng, bank)
                return last
            return copy

        def cols(a, b, rows=P):
            return lambda bank: bank[:rows, a:b]

        class MixerA:
            def __init__(self):
                c = Carve()
                w0 = c(DC, 768)
                self.w = [w0, aT[:], w0]
                self.q = c(AH, TOK)
                self.k = c(2, TOK)
                self.v = c(8, AH * HD)
                self.bias = [c(AH, 384), c(AH, P), c(AH, P)]
                self.stage = c(2, OROW)
                self.table = c(12)
                self.onehot = c(1024)
                self.f = c(1024)
                self.att = Attention("a", c, bias=True)
                self.groups = c(GROUPS, NT, OROW)
                self.a = c(NT, AH * HD)
                self.tmp = c(NT, AH * HD)
                self.m = c(NT, AH)
                self.wt = c(GROUPS, NT, AH)
                self.dn = c(NT, AH)
                self.t4 = c(NT, AH)
                self.proj = Project("a")
                self.zeroed = sem("a_zeroed")
                self.tabled = sem("a_tabled")
                self.mask_set = sem("a_mask_set")
                self.f_ready = sem("a_f_ready")
                self.f_out = sem("a_f_out")
                self.f_stored = sem("a_f_stored")
                self.shifted = sem("a_shifted")
                self.bias_in = sem("a_bias_in")
                self.w_in = [sem(f"a_w_in{i}") for i in range(2)]
                self.o_stored = [sem(f"a_o_stored{i}") for i in range(2)]
                self.groups_in = sem("a_groups_in")
                self.chain = sem("a_chain")
                self.joined = sem("a_joined")
                self.turned = slots("a_turned")
                self.turned_in = slots("a_turned_in")
                self.scale = HD ** -0.5
                self.units = [units_a(g) for g in range(GROUPS)]
                self.u0 = [sum(len(u) for u in self.units[:g]) for g in range(GROUPS)]
                self.t0 = [sum(self.tiles(h) for h in range(g)) for g in range(GROUPS)]
                for g in range(GROUPS):
                    assert len(self.units[g]) % 2 == 0 and self.tiles(g) % 2 == 0

            def tiles(self, g):
                return 6 if g == 0 else 8

            def blocks(self, g):
                out = []
                for part in (0, 1):
                    for pair in (0, 1):
                        for s in (0, HALF):
                            at = part * 256 + pair * P
                            out.append(product(cols(0, HALF), lambda c, at=at: self.w[g][:, c, at:at + P],
                                               lambda c, s=s: hT[:, c, s:s + HALF], DC))
                for ts in self.v_blocks(g):
                    rows = P if g == 0 or ts[0] < 4 else HD
                    out.append(wide(*[product(cols(i * 256, (i + 1) * 256, rows), lambda c, t=t: tokens_a(hT[:, c], g, t),
                                              lambda c: self.w[g][:, c, 512:768], DC) for i, t in enumerate(ts)]))
                return out

            def v_blocks(self, g):
                return [[0, 1], [2, 3], [4], [5]] if g == 0 else [[0, 1], [2, 3], [4, 5], [6, 7]]

            def copies(self, g):
                out = []
                for pair in (0, 1):
                    for s in (0, HALF):
                        out.append(split_heads(lambda h, pair=pair, s=s: self.q[:, 2 * pair + h, s:s + HALF], self.scale))
                for pair in (0, 1):
                    for s in (0, HALF):
                        out.append(copy_to(self.k[:, pair, s:s + HALF], cols(0, HALF)))
                for ts in self.v_blocks(g):
                    rows = P if g == 0 or ts[0] < 4 else HD
                    out.append(copy_to(self.v[:rows, ts[0]:ts[-1] + 1].rearrange("p t n -> p (t n)"), cols(0, 256 * len(ts), rows)))
                return out

            def half(self, g):
                return 6 * g

            def q_of(self, g):
                return lambda u, h: tokens_a(self.q[:, h], g, u.tile)

            def k_of(self, g):
                def k(u, h):
                    ap = self.k[:, h // 2]
                    if g == 0:
                        return ap[:, u.tiles[0] * P:(u.tiles[-1] + 1) * P]
                    return tokens_a(ap, g, u.tile)
                return k

            def bias_of(self, g):
                def bias(u, h):
                    if g == 0:
                        at = P if u.first_key == 0 else 0
                        return self.bias[0][:u.nq, h, at:at + u.nk]
                    return self.bias[g][:u.nq, h, :u.nk]
                return bias

            def sp_early(self, sp):
                sp.dma_start(self.table[0:32, :], t5).then_inc(self.tabled, 16)
                sp.dma_start(self.onehot[0:33, :], onehot).then_inc(self.tabled, 16)
                sp.dma_start(self.w[0], w_a[0]).then_inc(self.w_in[0], 16)

            def sp(self, sp):
                sp.dma_start(self.w[1], w_a[1]).then_inc(self.w_in[1], 16)
                sp.wait_ge(self.f_out, 2)
                sp.dma_start(f_dram, self.f[0:12, :]).then_inc(self.f_stored, 16)
                sp.wait_ge(self.f_stored, 16)
                with sp.Fori(0, CB) as b:
                    sp.dma_start(shifted_dram[b], f_dram[:, bass.ds(CB - 1 - b, 1024 - CB)]).then_inc(self.shifted, 16)
                sp.wait_ge(self.shifted, 16 * CB)
                for g, (at, n) in enumerate(((0, 384), (512, P), (768, P))):
                    for a in range(P // CB):
                        first = at + P - CB - CB * a
                        sp.dma_start(self.bias[g][a * CB:(a + 1) * CB], shifted_dram[:, AH * g:AH * (g + 1), first:first + n]
                                     ).then_inc(self.bias_in, 16)
                for g in range(GROUPS):
                    if g == 1:
                        sp.wait_ge(self.proj.ready, after(11))
                        sp.dma_start(self.w[2], w_a[2]).then_inc(self.w_in[0], 16)
                    if g == 2:
                        sp.wait_ge(self.proj.ready, after(35))
                        sp.dma_start(mix_b.w, w_b).then_inc(mix_b.w_in, 16)
                    tile = 0
                    for j, u in enumerate(self.units[g]):
                        if not u.last:
                            continue
                        sp.wait_ge(self.att.o_out, after(self.u0[g] + j))
                        rows = oa_dram[g].rearrange("t n -> n t")
                        dst = tokens_a(rows, g, u.tile)
                        dst = dst.rearrange("n t -> t n")
                        sp.dma_start(dst, self.stage[:u.nq, tile % 2]).then_inc(self.o_stored[tile % 2], 16)
                        tile += 1

            def stored(self, eng, tiles):
                for par in range(2):
                    if (n := (tiles + 1 - par) // 2) > 0:
                        eng.wait_ge(self.o_stored[par], 16 * n)

            def out_of(self, g):
                def out(dve, u, j, u0, t0, tile, o):
                    k, h0, s = len(u.heads), u.heads[0], self.stage[:u.nq, tile % 2].rearrange("p (h c) -> p h c", h=AH)
                    n = self.t0[g] + tile
                    if n >= 2:
                        dve.wait_ge(self.o_stored[tile % 2], 16 * (n // 2))
                    dve.tensor_copy(s[:, h0:h0 + k, HD], smax[:u.nq, j, :k])
                    dve.tensor_copy(s[:, h0:h0 + k, HD + 1], den[:u.nq, j, :k])
                    dve.tensor_copy(s[:, h0:h0 + k, 0:HD], o.rearrange("p (h c) -> p h c", h=k)).then_inc(self.att.o_out, 1)
                return out

            def pe(self, pe):
                pe.wait_ge(self.tabled, 32)
                pe.wait_ge(self.mask_set, 1)
                for b in range(2):
                    pe.matmul(score_ps[0:12, b, :], self.table[0:33, :], self.onehot[0:33, b * 512:(b + 1) * 512],
                              start=True, stop=True).then_inc(self.f_ready, 1)
                pe.wait_ge(self.f_out, 2)
                pe.wait_ge(self.w_in[0], 16)
                self.proj.pe(pe, self.blocks(0), 0)
                for g in range(GROUPS):
                    self.proj.all_out(pe, self.half(g) + 6)
                    v = lambda u, h, t: self.v[:u.kt, t, h * HD:(h + 1) * HD]

                    def beside(d):
                        if d == 0:
                            pe.wait_ge(self.w_in[(g + 1) % 2], 32 if g + 1 == 2 else 16)
                        self.proj.pe_one(pe, self.blocks(g + 1), self.half(g + 1), d)

                    more = g + 1 < GROUPS
                    self.att.pe(pe, self.units[g], self.u0[g], self.t0[g], self.q_of(g), self.k_of(g), v, None, beside if more else None)
                    if more:
                        self.proj.pe(pe, self.blocks(g + 1), self.half(g + 1), first=4)

            def act(self, act):
                act.wait_ge(self.zeroed, 1)
                self.proj.out(act, 0, self.copies(0), 0)
                for g in range(GROUPS):
                    if g + 1 < GROUPS:
                        copies, h0 = self.copies(g + 1), self.half(g + 1)
                        self.att.act(act, self.units[g], self.u0[g], self.proj.act_beside(act, copies, h0))
                        self.proj.out(act, 0, copies, h0, first=4)
                    else:
                        self.att.act(act, self.units[g], self.u0[g])

            def dve_early(self, dve):
                dve.memset(self.table[32:33, :], MASKED).then_inc(self.mask_set, 1)
                dve.memset(self.q, 0.0).then_inc(self.zeroed, 1)

            def dve(self, dve):
                dve.wait_ge(self.zeroed, 1)
                for b in range(2):
                    dve.wait_ge(self.f_ready, b + 1)
                    dve.tensor_copy(self.f[0:12, b * 512:(b + 1) * 512], score_ps[0:12, b, :]).then_inc(self.f_out, 1)
                self.proj.out(dve, 1, self.copies(0), 0)
                dve.wait_ge(self.bias_in, 16 * GROUPS * (P // CB))
                for g in range(GROUPS):
                    args = (dve, self.units[g], self.u0[g], self.t0[g], self.bias_of(g), self.out_of(g), None)
                    if g + 1 < GROUPS:
                        copies, h0 = self.copies(g + 1), self.half(g + 1)
                        self.att.dve(*args, self.proj.dve_beside(dve, copies, h0))
                        self.proj.out(dve, 1, copies, h0, first=4)
                    else:
                        self.att.dve(*args)

            def join_sp(self, sp):
                for g in range(GROUPS):
                    sp.dma_start(self.groups[:, g], oa_dram[g].rearrange("(t p) n -> p t n", p=P)).then_inc(self.groups_in, 16)

            def join_dve(self, dve, latent_copy):
                steps = [0]

                def step(ins):
                    steps[0] += 1
                    ins.then_inc(self.chain, 1)
                    dve.wait_ge(self.chain, steps[0])

                dve.wait_ge(self.groups_in, 16 * GROUPS)
                g = [self.groups[:, i].rearrange("p t (h c) -> p t h c", h=AH) for i in range(GROUPS)]
                step(dve.tensor_tensor(self.m, g[0][:, :, :, HD], g[1][:, :, :, HD], ALU.max))
                step(dve.tensor_tensor(self.m, self.m, g[2][:, :, :, HD], ALU.max))
                for i in range(GROUPS):
                    step(dve.tensor_tensor(self.wt[:, i], g[i][:, :, :, HD], self.m, ALU.subtract))
                dve.tensor_copy(self.t4, self.m).then_inc(self.joined, 1)
                dve.wait_ge(self.joined, 2)
                step(dve.tensor_tensor(self.dn, self.wt[:, 0], g[0][:, :, :, HD + 1], ALU.mult))
                for i in (1, 2):
                    step(dve.tensor_tensor(self.t4, self.wt[:, i], g[i][:, :, :, HD + 1], ALU.mult))
                    step(dve.tensor_tensor(self.dn, self.dn, self.t4, ALU.add))
                step(dve.reciprocal(self.dn, self.dn))
                for i in range(GROUPS):
                    step(dve.tensor_tensor(self.wt[:, i], self.wt[:, i], self.dn, ALU.mult))
                for t in range(NT):
                    latent_copy(dve, t)
                    a = self.a[:, t].rearrange("p (h c) -> p h c", h=AH)
                    tmp = self.tmp[:, t].rearrange("p (h c) -> p h c", h=AH)
                    w = [self.wt[:, i, t].unsqueeze(2).to_broadcast([P, AH, HD]) for i in range(GROUPS)]
                    step(dve.tensor_tensor(a, g[0][:, t, :, 0:HD], w[0], ALU.mult))
                    for i in (1, 2):
                        step(dve.tensor_tensor(tmp, g[i][:, t, :, 0:HD], w[i], ALU.mult))
                        step(dve.tensor_tensor(a, a, tmp, ALU.add))
                dve.sem_inc(self.joined, 1)
                for t in range(NT):
                    dve.wait_ge(self.turned, after(t))
                    dve.tensor_copy(aT[:, 0:2, t * P:(t + 1) * P],
                                    score_ps[:, t % 2, 0:256].rearrange("p (c t) -> p c t", c=2)).then_inc(self.turned_in, 1)

            def join_act(self, act):
                act.wait_ge(self.joined, 1)
                act.activation(self.wt, self.wt, ACT.Exp).then_inc(self.joined, 1)

            def join_pe(self, pe):
                pe.wait_ge(self.joined, 3)
                for t in range(NT):
                    pe.wait_ge(self.turned_in, after(t - 2))
                    for c in range(2):
                        last = pe.transpose(score_ps[:, t % 2, c * P:(c + 1) * P], self.a[:, t, c * P:(c + 1) * P], ident[:])
                    last.then_inc(self.turned, 1)

        class MixerB:
            def __init__(self):
                c = Carve()
                self.w = c(DC, B_IN)
                self.u = c(NT, B_IN)
                self.junk = c(QR)
                self.kk = c(NT, P)
                self.rope = c(NT, 2, ROPE // 2)
                self.rt = c(4, NT, ROPE // 2)
                self.cq = c(3, TOK)
                self.ckv = c(2, TOK)
                self.wq = c(3, 256)
                self.wkv = c(2, 256)
                self.q_table = c(TOK)
                self.q = c(2, TOK)
                self.k = c(2, TOK)
                self.v = c(NT, P)
                self.o_sb = c(2, P)
                self.att = Attention("b", c, bias=False)
                self.proj = Project("b")
                self.lat = Project("b_latent")
                self.units = units_b()
                self.tiles = NT
                self.w_in = sem("b_w_in")
                self.tables_in = sem("b_tables_in")
                self.squares = sem("b_squares")
                self.mean = sem("b_mean")
                self.chain = sem("b_chain")
                self.scaled = sem("b_scaled")
                self.turned = slots("b_turned")
                self.turned_act = slots("b_turned_act")
                self.turned_dve = slots("b_turned_dve")
                self.pair_in = sem("b_pair_in")
                self.v_blocks = [[0, 1, 2], [3, 4, 5]]

            def latent_blocks(self):
                return [product(cols(0, n), lambda c, t=t: hT[:, c, t * P:(t + 1) * P], lambda c, a=a, n=n: self.w[:, c, a:a + n], DC)
                        for t in range(NT) for a, n in ((0, QR), (QR, KVR + ROPE))]

            def latent_copies(self):
                return [copy_to(self.u[:, t, a:a + n], cols(0, n)) for t in range(NT) for a, n in ((0, QR), (QR, KVR + ROPE))]

            def blocks(self):
                halves = (0, HALF)
                q = [product(cols(0, HALF), lambda c, h=h: self.wq[:, c, h * P:(h + 1) * P],
                             lambda c, s=s: self.cq[:, c, s:s + HALF], 3) for h in (0, 1) for s in halves]
                k = [product(cols(0, HALF), lambda c: self.wkv[:, c, 0:P], lambda c, s=s: self.ckv[:, c, s:s + HALF], 2) for s in halves]
                v = [wide(*[product(cols(i * P, (i + 1) * P), lambda c, t=t: self.ckv[:, c, t * P:(t + 1) * P],
                                    lambda c: self.wkv[:, c, P:2 * P], 2) for i, t in enumerate(ts)]) for ts in self.v_blocks]
                return [k[0], q[0], k[1], q[1], v[0], q[2], v[1], q[3]]

            def copies(self):
                def k_copy(s):
                    def copy(act, bank):
                        act.activation(self.k[0:HD, 0, s:s + HALF], bank[0:HD, 0:HALF], ACT.Copy)
                        return act.activation(self.k[0:HD, 1, s:s + HALF], bank[HD:P, 0:HALF], ACT.Copy)
                    return copy

                def q_copy(h, s):
                    return lambda dve, bank: dve.tensor_tensor(self.q[:, h, s:s + HALF], bank[:, 0:HALF],
                                                               self.q_table[:, s:s + HALF], ALU.mult)
                v = [copy_to(self.v[:, ts[0]:ts[-1] + 1].rearrange("p t n -> p (t n)"), cols(0, HALF)) for ts in self.v_blocks]
                return [k_copy(0), q_copy(0, 0), k_copy(HALF), q_copy(0, HALF), v[0], q_copy(1, 0), v[1], q_copy(1, HALF)]

            def sp_early(self, sp):
                sp.dma_start(self.q_table, q_table).then_inc(self.tables_in, 16)
                sp.dma_start(self.rope, rope_in).then_inc(self.tables_in, 16)
                sp.dma_start(self.wq, w_qb[0]).then_inc(self.pair_in, 16)
                sp.dma_start(self.wkv, w_kvb[0]).then_inc(self.pair_in, 16)

            def sp(self, sp):
                with sp.Fori(1, B_PAIRS) as i:
                    sp.wait_ge(self.proj.ready, after(8 * i - 1))
                    sp.dma_start(self.wq, w_qb[i]).then_inc(self.pair_in, 16)
                    sp.dma_start(self.wkv, w_kvb[i]).then_inc(self.pair_in, 16)

            def latent_pe(self, pe):
                pe.wait_ge(self.w_in, 16)
                self.lat.pe(pe, self.latent_blocks(), 0)

            def latent_act(self, act):
                copies = self.latent_copies()
                for t in range(NT + 1):
                    if t < NT:
                        self.lat.out_one(act, copies, 0, 2 * t)
                    if t:
                        self.latent_squares(act, t - 1)

            def latent_squares(self, act, t):
                act.wait_ge(self.lat.act_out, after(t))
                act.wait_ge(self.lat.dve_out, after(t))
                for i, (a, n) in enumerate(((0, QR), (QR, KVR))):
                    if 2 * t + i:
                        act.wait_ge(self.squares, 2 * t + i)
                    act.activation(self.junk[:, :n], self.u[:, t, a:a + n], ACT.Square,
                                   accum_out=bstat[:, i, t:t + 1]).then_inc(self.squares, 1)

            def latent_dve(self, dve, t):
                dve.wait_ge(self.lat.ready, after(2 * t + 1))
                self.latent_copies()[2 * t + 1](dve, proj_ps[:, 1]).then_inc(self.lat.dve_out, 1)

            def pe(self, pe):
                pe.wait_ge(self.scaled, 1)
                for t in range(NT):
                    for part in range(2):
                        pe.wait_ge((self.turned_act, self.turned_dve)[part], after(t - 1))
                        srcs = [self.u[:, t, c * P:(c + 1) * P] for c in range(3)] + [self.kk[:, t]] if part == 0 else \
                               [self.u[:, t, QR + c * P:QR + (c + 1) * P] for c in range(2)]
                        for i, s in enumerate(srcs):
                            last = pe.transpose(proj_ps[:, part, i * P:(i + 1) * P], s, ident[:])
                        last.then_inc(self.turned, 1)
                pe.wait_ge(self.turned_act, after(NT - 1))
                pe.wait_ge(self.turned_dve, after(NT - 1))
                pe.wait_ge(self.pair_in, 32)
                self.proj.pe(pe, self.blocks(), 0)
                with pe.Fori(0, B_PAIRS - 1) as i:
                    self.pe_pair(pe, i)
                self.pe_pair(pe, B_PAIRS - 1, last=True)

            def pe_pair(self, pe, i, last=False):
                def beside(d):
                    if d == 0:
                        pe.wait_ge(self.pair_in, 32 * i + 64)
                    self.proj.pe_one(pe, self.blocks(), 4 * i + 4, d)

                self.proj.all_out(pe, 4 * i + 4)
                v = lambda u, h, t: self.v[:, t, h * HD:(h + 1) * HD]
                self.att.pe(pe, self.units, len(self.units) * i, self.tiles * i,
                            lambda u, h: self.q[:, h, u.tile * P:(u.tile + 1) * P],
                            lambda u, h: self.k[:, h, u.tiles[0] * P:(u.tiles[-1] + 1) * P], v, self.o_sb, None if last else beside)
                if not last:
                    self.proj.pe(pe, self.blocks(), 4 * i + 4, first=4)

            def act(self, act):
                act.wait_ge(self.mean, 1)
                act.activation(brstd[:], brstd[:], ACT.Sqrt).then_inc(self.mean, 1)
                for t in range(NT):
                    act.wait_ge(self.turned, after(2 * t))
                    for c in range(3):
                        last = act.activation(self.cq[:, c, t * P:(t + 1) * P], proj_ps[:, 0, c * P:(c + 1) * P], ACT.Copy,
                                              scale=gq[:, c:c + 1])
                    for h in range(2):
                        last = act.activation(self.k[HD:P, h, t * P:(t + 1) * P], proj_ps[HD:P, 0, 3 * P:4 * P], ACT.Copy)
                    last.then_inc(self.turned_act, 1)
                self.proj.out(act, 0, self.copies(), 0)
                n = len(self.units)
                with act.Fori(0, B_PAIRS - 1) as i:
                    self.att.act(act, self.units, n * i, self.proj.act_beside(act, self.copies(), 4 * i + 4))
                    self.proj.out(act, 0, self.copies(), 4 * i + 4, first=4)
                self.att.act(act, self.units, n * (B_PAIRS - 1))

            def dve(self, dve):
                dve.memset(self.kk, 0.0)
                steps = [0]

                def step(ins):
                    steps[0] += 1
                    ins.then_inc(self.chain, 1)
                    dve.wait_ge(self.chain, steps[0])

                dve.wait_ge(self.squares, 2 * NT)
                dve.tensor_scalar(brstd[:, 0], bstat[:, 0], 1.0 / QR, EPS, ALU.mult, ALU.add)
                dve.tensor_scalar(brstd[:, 1], bstat[:, 1], 1.0 / KVR, EPS, ALU.mult, ALU.add).then_inc(self.mean, 1)
                dve.wait_ge(self.mean, 2)
                step(dve.reciprocal(brstd[:], brstd[:]))
                dve.wait_ge(self.tables_in, 32)
                R = ROPE // 2
                k1, k2 = self.u[:, :, QR + KVR:QR + KVR + R], self.u[:, :, QR + KVR + R:B_IN]
                cos, sin = self.rope[:, :, 0], self.rope[:, :, 1]
                for i, (a, b) in enumerate(((k1, cos), (k2, sin), (k2, cos), (k1, sin))):
                    last = dve.tensor_tensor(self.rt[:, i], a, b, ALU.mult)
                step(last)
                for twice in range(2):
                    at = HD + twice * ROPE
                    dve.tensor_tensor(self.kk[:, :, at:at + R], self.rt[:, 0], self.rt[:, 1], ALU.subtract)
                    dve.tensor_tensor(self.kk[:, :, at + R:at + 2 * R], self.rt[:, 2], self.rt[:, 3], ALU.add)
                for t in range(NT):
                    for i, (a, n) in enumerate(((0, QR), (QR, KVR))):
                        last = dve.tensor_scalar(self.u[:, t, a:a + n], self.u[:, t, a:a + n], brstd[:, i, t:t + 1], None, ALU.mult)
                last.then_inc(self.scaled, 1)
                for t in range(NT):
                    dve.wait_ge(self.turned, after(2 * t + 1))
                    dve.tensor_tensor(self.ckv[:, :, t * P:(t + 1) * P], proj_ps[:, 1, 0:256].rearrange("p (c t) -> p c t", c=2),
                                      gkv.unsqueeze(2).to_broadcast([P, 2, P]), ALU.mult).then_inc(self.turned_dve, 1)
                self.proj.out(dve, 1, self.copies(), 0)

                def attend(i, beside=None):
                    self.att.dve(dve, self.units, len(self.units) * i, self.tiles * i, None, self.att.normalised(self.o_sb),
                                 lambda u: aT[:, i + 2, u.tile * P:(u.tile + 1) * P], beside)

                with dve.Fori(0, B_PAIRS - 1) as i:
                    attend(i, self.proj.dve_beside(dve, self.copies(), 4 * i + 4))
                    self.proj.out(dve, 1, self.copies(), 4 * i + 4, first=4)
                attend(B_PAIRS - 1)

        class MixerC:

            def __init__(self):
                c = Carve()
                self.w = c(DC, 2 * P)
                self.q = c(2, TOK)
                self.k = c(TOK)
                self.v = c(2 * NB, 2 * P)
                self.window = c(2, C_ROWS, WIN)
                self.bias = c(2, 7, C_ROWS, CB)
                self.mask = c(7, CB)
                self.o_sb = c(2, P)
                self.att = Attention("c", c, bias=True)
                assert c.at <= C_PARTS_AT
                self.w1 = Carve(c.at - DC * 2 * P)(DC, 2 * P)
                self.proj = Project("c")
                self.zeroed = sem("c_zeroed")
                self.units = units_c()
                self.tiles = 2 * NB
                self.windows_out = sem("c_windows_out")
                self.mask_in = sem("c_mask_in")
                self.w_in = sem("c_w_in")
                self.w1_in = sem("c_w1_in")
                self.w_hi = slots("c_w_hi")
                self.w_lo = slots("c_w_lo")
                self.window_in = sem("c_window_in")
                self.biased = slots("c_biased")
                self.scale = HD ** -0.5
                assert len(self.units) == 10

            def windows(self, sp):
                with sp.Fori(0, CB) as c:
                    sp.dma_start(window_dram[c], rpb[:, :, bass.ds(CB - 1 - c, WIN)]).then_inc(self.windows_out, 16)

            def blocks(self):
                h = lambda c, s: (n_hi[:, c, s:s + HALF], n_lo[:, c, s:s + HALF])
                return [product3(cols(0, HALF), lambda c, a=a: (qk_hi[:, c, a:a + P], qk_lo[:, c, a:a + P]), lambda c, s=s: h(c, s), DC)
                        for a in (0, P) for s in (0, HALF)]

            def v_blocks(self):
                h = lambda c, t: (n_hi[:, c, t:t + P], n_lo[:, c, t:t + P])
                one = lambda t, at: product3(cols(at, at + 2 * P), lambda c: h(c, t), lambda c: (v_hi[:, c], v_lo[:, c]), DC)
                return [wide(one(0, 0), one(P, 2 * P)), wide(one(2 * P, 0), one(3 * P, 2 * P)), one(PROMPT, 0), one(PROMPT + P, 0)]

            def copies(self):
                out = [split_heads(lambda h, s=s: self.q[:, h, s:s + HALF], self.scale) for s in (0, HALF)]
                out += [copy_to(self.k[:, s:s + HALF], cols(0, HALF)) for s in (0, HALF)]
                return out

            def v_copies(self):
                def sample_v(i):
                    def copy(eng, bank):
                        rows = CB * S_ROWS
                        for k in range(2):
                            last = copy_to(self.v[:rows, NB + 2 * i + k], lambda bank: bank[k * rows:(k + 1) * rows, 0:2 * P])(eng, bank)
                        return last
                    return copy
                prompt_v = [copy_to(self.v[:, 2 * i:2 * i + 2].rearrange("p t n -> p (t n)"), cols(0, 512)) for i in range(2)]
                return prompt_v + [sample_v(0), sample_v(1)]

            def window_loads(self, sp, i):
                for r in range(C_ROWS):
                    sp.dma_start(self.window[r * CB:(r + 1) * CB], window_dram[:, bass.ds(2 * i, 2), C_ROWS - 1 - r:2 * C_ROWS - 1 - r]
                                 ).then_inc(self.window_in, 16)

            def load(self, sp, n):
                sp.wait_ge(self.w_lo, after(n - 1))
                sp.dma_start(self.w, w_c[n]).then_inc(self.w_in, 16)

            def sp_first(self, sp):
                sp.dma_start(self.w, w_c[0]).then_inc(self.w_in, 16)
                sp.dma_start(self.w1, w_c[1]).then_inc(self.w1_in, 16)

            def sp_early(self, sp):
                sp.dma_start(self.mask, col_mask).then_inc(self.mask_in, 16)
                sp.wait_ge(self.windows_out, 16 * CB)
                self.window_loads(sp, 0)

            def sp_couple(self, sp, c, last=False):
                self.load(sp, 3 * c + 2)
                sp.wait_ge(self.biased, after(2 * c))
                self.window_loads(sp, 2 * c + 1)
                if not last:
                    self.load(sp, 3 * c + 3)
                    self.load(sp, 3 * c + 4)
                    sp.wait_ge(self.biased, after(2 * c + 1))
                    self.window_loads(sp, 2 * c + 2)

            def sp(self, sp):
                with sp.Fori(0, C_PAIRS // 2 - 1) as c:
                    self.sp_couple(sp, c)
                self.sp_couple(sp, C_PAIRS // 2 - 1, last=True)

            def split_hi(self, act, n, dst):
                act.wait_ge(self.w_in, 16 * n)
                act.activation(dst[:], self.w, ACT.Copy).then_inc(self.w_hi, 1)

            def split_lo(self, pool, n, hi, dst, src=None):
                pool.wait_ge(self.w_hi, after(n))
                pool.tensor_tensor(dst[:], self.w if src is None else src, hi[:].bitcast(F32), ALU.subtract).then_inc(self.w_lo, 1)

            def make_bias(self, pool, i):
                pool.wait_ge(self.window_in, 16 * C_ROWS * i + 16 * C_ROWS)
                pool.wait_ge(self.att.maxed, after(len(self.units) * i - 1))
                for h in range(2):
                    win = self.window[:, h].rearrange("p r (b c) -> p b r c", c=CB)
                    for b0, n, d0 in ((0, 2, 1), (2, 3, 0), (5, 2, 0)):
                        last = pool.tensor_tensor(self.bias[:, h, b0:b0 + n], win[:, d0:d0 + n],
                                                  self.mask[:, b0:b0 + n].unsqueeze(2).to_broadcast([P, n, C_ROWS, CB]), ALU.add)
                last.then_inc(self.biased, 1)


            def pool_early(self, pool):
                self.split_lo(pool, 0, v_hi, v_lo)
                self.split_lo(pool, 1, qk_hi, qk_lo, self.w1)

            def act_early_v(self, act):
                act.wait_ge(self.w_in, 16)
                act.activation(v_hi[:], self.w, ACT.Copy).then_inc(self.w_hi, 1)

            def act_early_qk(self, act):
                act.wait_ge(self.w1_in, 16)
                act.activation(qk_hi[:], self.w1, ACT.Copy).then_inc(self.w_hi, 1)

            def pool_couple(self, pool, c, last=False):
                self.make_bias(pool, 2 * c)
                self.split_lo(pool, 3 * c + 2, qk_hi, qk_lo)
                if not last:
                    self.split_lo(pool, 3 * c + 3, v_hi, v_lo)
                self.make_bias(pool, 2 * c + 1)
                if not last:
                    self.split_lo(pool, 3 * c + 4, qk_hi, qk_lo)

            def pool(self, pool):
                pool.wait_ge(self.mask_in, 16)
                with pool.Fori(0, C_PAIRS // 2 - 1) as c:
                    self.pool_couple(pool, c)
                self.pool_couple(pool, C_PAIRS // 2 - 1, last=True)

            def bias_of(self, u, h):
                at, n = C_BIAS0[u.first_key], len(u.tiles)
                if u.tile < NB:
                    return self.bias[:, h, at:at + n].rearrange("p b r c -> p (b r c)")
                return self.bias[:u.nq, h, at:at + n, 0:S_ROWS].rearrange("p b r c -> p b (r c)")

            def pe_pair(self, pe, c, par, last=False):
                pair, h0 = 2 * c + par, 6 * c + (4 if par == 0 else 6)
                v_next = par == 1
                blocks = self.blocks() + (self.v_blocks() if v_next else [])

                def beside(d):
                    if d == 0:
                        pe.wait_ge(self.w_lo, after(3 * c + 2 + 2 * par))
                    self.proj.pe_one(pe, blocks, h0, d)

                self.proj.all_out(pe, h0)
                v = lambda u, h, t: self.v[:u.kt, t, (2 * par + h) * HD:(2 * par + h + 1) * HD]
                self.att.pe(pe, self.units, len(self.units) * pair, self.tiles * pair,
                            lambda u, h: run_c(self.q[:, h], u.tile),
                            lambda u, h: run_c(self.k, u.tiles[0], len(u.tiles)), v, self.o_sb, None if last else beside)
                if v_next and not last:
                    self.proj.pe(pe, blocks, h0, first=4)

            def pe(self, pe):
                pe.wait_ge(self.w_lo, after(1))
                self.proj.pe(pe, self.blocks() + self.v_blocks(), 0)
                with pe.Fori(0, C_PAIRS // 2 - 1) as c:
                    self.pe_pair(pe, c, 0)
                    self.pe_pair(pe, c, 1)
                self.pe_pair(pe, C_PAIRS // 2 - 1, 0)
                self.pe_pair(pe, C_PAIRS // 2 - 1, 1, last=True)

            def act_couple(self, act, c, last=False):
                n = len(self.units)
                act.wait_ge(self.proj.ready, after(12 * c + 7))
                self.split_hi(act, 3 * c + 2, qk_hi)
                self.att.act(act, self.units, n * 2 * c, self.proj.act_beside(act, self.copies(), 6 * c + 4),
                             None if last else lambda: self.split_hi(act, 3 * c + 3, v_hi))
                if last:
                    self.att.act(act, self.units, n * (2 * c + 1))
                    return
                act.wait_ge(self.proj.ready, after(12 * c + 11))
                self.split_hi(act, 3 * c + 4, qk_hi)
                copies = self.copies() + self.v_copies()
                self.att.act(act, self.units, n * (2 * c + 1), self.proj.act_beside(act, copies, 6 * c + 6))
                self.proj.out(act, 0, copies, 6 * c + 6, first=4)

            def act(self, act):
                act.wait_ge(self.zeroed, 1)
                self.proj.out(act, 0, self.copies() + self.v_copies(), 0)
                with act.Fori(0, C_PAIRS // 2 - 1) as c:
                    self.act_couple(act, c)
                self.act_couple(act, C_PAIRS // 2 - 1, last=True)

            def dve_early(self, dve):
                dve.memset(self.q, 0.0).then_inc(self.zeroed, 1)

            def dve(self, dve):
                dve.wait_ge(self.zeroed, 1)
                n, copies = len(self.units), self.copies() + self.v_copies()
                self.proj.out(dve, 1, copies, 0)

                def attend(c, par, beside=None):
                    pair = 2 * c + par
                    dve.wait_ge(self.biased, after(pair))
                    self.att.dve(dve, self.units, n * pair, self.tiles * pair, self.bias_of, self.att.normalised(self.o_sb),
                                 lambda u: tokens_c(aT[:, pair], u.tile), beside)

                with dve.Fori(0, C_PAIRS // 2 - 1) as c:
                    attend(c, 0, self.proj.dve_beside(dve, copies, 6 * c + 4))
                    attend(c, 1, self.proj.dve_beside(dve, copies, 6 * c + 6))
                    self.proj.out(dve, 1, copies, 6 * c + 6, first=4)
                c = C_PAIRS // 2 - 1
                attend(c, 0, self.proj.dve_beside(dve, copies, 6 * c + 4))
                attend(c, 1)

        class OutProject:

            def __init__(self, l):
                self.l = l
                self.w = Carve(ARENA - DC * D)(DC, D)
                a = [(aT[:, :, t * P:(t + 1) * P], n_hi[:, :, t * P:(t + 1) * P], n_lo[:, :, t * P:(t + 1) * P]) for t in range(NT)]
                w = lambda h, c: tuple(m[:, c:c + DC // 2, h * 512:(h + 1) * 512] for m in (self.w, wo_hi, wo_lo))
                self.pieces = [a[0], w(0, 0), w(0, DC // 2), *a[1:], w(1, 0), w(1, DC // 2)]

            def sp(self, sp):
                sp.dma_start(self.w, w_out[self.l]).then_inc(out_w_in, 16)

            def pe(self, pe):
                for n in range(2 * NT):
                    t, half = n % NT, n // NT
                    pe.wait_ge(out_added, after(2 * NT * self.l + n - 2))
                    for c in range(DC):
                        if c % (DC // 2) == 0:
                            first = c == 0 and t == 0
                            done = (2 if first else 3 + t) if half == 0 else len(self.pieces) - first
                            pe.wait_ge(out_lo, len(self.pieces) * self.l + done)
                        for k, (a, w) in enumerate(((n_hi, wo_hi), (n_lo, wo_hi), (n_hi, wo_lo))):
                            last = pe.matmul(proj_ps[:, n % 2], a[:, c, t * P:(t + 1) * P], w[:, c, half * 512:(half + 1) * 512],
                                             start=(c == 0 and k == 0), stop=(c == DC - 1 and k == 2))
                    last.then_inc(out_ready, 1)

            def act(self, act):
                act.wait_ge(out_w_in, 16 * (self.l + 1))
                for raw, hi, _ in self.pieces:
                    act.activation(hi, raw, ACT.Copy).then_inc(out_hi, 1)

            def split_lo(self, dve, i):
                raw, hi, lo = self.pieces[i]
                dve.wait_ge(out_hi, len(self.pieces) * self.l + i + 1)
                dve.tensor_tensor(lo, raw, hi.bitcast(F32), ALU.subtract).then_inc(out_lo, 1)

            def dve(self, dve):
                for i in (0, 1, 2):
                    self.split_lo(dve, i)
                for n in range(2 * NT):
                    t, half = n % NT, n // NT
                    for i in {0: (3, 4), 1: (5,), 2: (6,), 3: (7, 8), 4: (9,)}.get(n, ()):
                        self.split_lo(dve, i)
                    dve.wait_ge(out_ready, after(2 * NT * self.l + n))
                    xs = x[:, t, half * 512:(half + 1) * 512]
                    dve.tensor_tensor(xs, xs, proj_ps[:, n % 2], ALU.add).then_inc(out_added, 1)

        out_hi, out_lo = sem("out_hi"), sem("out_lo")
        out_w_in = sem("out_w_in")
        out_ready = slots("out_ready")
        out_added = slots("out_added")

        class Route:
            def __init__(self, l):
                self.l = l
                c = Carve(3 * DC * FF)
                self.z = c(NT, NE)
                self.z2 = c(NT, NE)
                self.m = c(NT)
                self.work = c(PROMPT)
                self.vals = c(CAP_P)
                self.idx = c(CAP_P).bitcast(U32)
                self.idx_f = c(CAP_P)
                self.idxT = idxT[:, NE * l:NE * l + NE]
                self.gateT = gateT[:, NE * l:NE * l + NE]
            def pe_logits(self, pe, t):
                for c in range(DC):
                    last = pe.matmul(pT_ps[:, 0, t * NE:(t + 1) * NE], hT[:, c, t * P:(t + 1) * P], router_sb[:, self.l, c],
                                     start=(c == 0), stop=(c == DC - 1))
                last.then_inc(route_logits, 1)

            def pe(self, pe):
                pe.wait_ge(route_aff, self.l + 1)
                for t in range(NT):
                    last = pe.transpose(score_ps[:NE, t // 4, (t % 4) * P:(t % 4 + 1) * P], self.z[:, t], ident[:])
                last.then_inc(route_turned, 1)
                pe.wait_ge(route_chosen, self.l + 1)
                pe.transpose(proj_ps[:CAP_P, 1, 0:S_END], self.idx_f[:S_END, :], ident[:S_END, :S_END])
                pe.transpose(proj_ps[:CAP_P, 1, S_END:2 * S_END], self.vals[:S_END, :], ident[:S_END, :S_END]).then_inc(route_lists, 1)

            def act(self, act):
                act.wait_ge(route_exped, 2 * self.l + 1)
                act.activation(self.z2, self.z2, ACT.Exp).then_inc(route_exped, 1)

            def dve(self, dve):
                steps = [0]

                def step(ins):
                    steps[0] += 1
                    ins.then_inc(route_chain, 1)
                    dve.wait_ge(route_chain, steps[0] + STEPS * self.l)

                dve.wait_ge(route_logits, NT * (self.l + 1))
                z = pT_ps[:, 0, 0:NT * NE].rearrange("p (t e) -> p t e", e=NE)
                wide_m = self.m.unsqueeze(2).to_broadcast([P, NT, NE])
                dve.memset(self.work[:S_END, :], -2.0)
                dve.memset(self.vals[:S_END, :], 0.0)
                step(dve.memset(self.idx_f[:S_END, :], 0.0))
                step(dve.tensor_reduce(self.m, z, AX.X, ALU.max))
                dve.tensor_tensor(self.z2, z, wide_m, ALU.subtract).then_inc(route_exped, 1)
                dve.wait_ge(route_exped, 2 * self.l + 2)
                step(dve.tensor_reduce(self.m, self.z2, AX.X, ALU.add))
                step(dve.reciprocal(self.m, self.m))
                dve.tensor_tensor(self.z, self.z2, wide_m, ALU.mult).then_inc(route_aff, 1)
                dve.wait_ge(route_turned, self.l + 1)
                step(dve.tensor_copy(self.work[:NE, :], score_ps[:NE, 0]))
                step(dve.tensor_copy(self.work[S_AT:S_END, 0:SAMPLE], score_ps[:NE, 1, 0:SAMPLE]))
                for r in range(0, CAP_P, 8):
                    rows = S_END if r < CAP_S else NE
                    left = self.work[:rows, :]
                    step(dve.max(self.vals[:rows, r:r + 8], left))
                    step(dve.max_index(self.idx[:rows, r:r + 8], self.vals[:rows, r:r + 8], left))
                    if r + 8 < CAP_P:
                        step(dve.match_replace(left, self.vals[:rows, r:r + 8], left, -1.0))
                dve.tensor_copy(self.idx_f[:S_AT, 0:CAP_S], self.idx[:S_AT, 0:CAP_S])
                dve.tensor_copy(self.idx_f[:NE, CAP_S:CAP_P], self.idx[:NE, CAP_S:CAP_P])
                dve.tensor_scalar(self.idx_f[S_AT:S_END, 0:CAP_S], self.idx[S_AT:S_END, 0:CAP_S], float(PROMPT), None,
                                  ALU.add).then_inc(route_chosen, 1)
                dve.wait_ge(route_lists, self.l + 1)
                for lists, at in ((self.idxT, 0), (self.gateT, S_END)):
                    dve.tensor_copy(lists[:CAP_P, :], proj_ps[:CAP_P, 1, at:at + NE])
                    dve.tensor_copy(lists[CAP_P:CAP, :], proj_ps[:CAP_S, 1, at + S_AT:at + S_END]).then_inc(route_lists_out, 1)
                assert steps[0] == STEPS

        STEPS = 5 + 3 * (CAP_P // 8)
        route_logits, route_exped, route_aff = sem("route_logits"), sem("route_exped"), sem("route_aff")
        route_turned, route_chosen, route_lists = sem("route_turned"), sem("route_chosen"), sem("route_lists")
        route_chain, route_lists_out = sem("route_chain"), sem("route_lists_out")

        idxT = sb("idxT", [P, 2 * NE], U32)
        gateT = sb("gateT", [P, 2 * NE])


        class Experts:

            def __init__(self):
                n = "moe"
                c = Carve()
                self.raw = c(RAW, SL, FF)
                self.xe = c(D)
                self.silu = c(FF)
                self.hid = c(FF)
                self.y = c(D)
                self.xeT = c(DC, CAP)
                self.gather_idx = sb(f"{n}_gather_idx", [P, 1], U32)
                self.scatter_idx = sb(f"{n}_scatter_idx", [P, 1], U32)
                self.w_in = [sem(f"{n}_w_in{s}") for s in range(RAW)]
                self.w_hi = slots(f"{n}_w_hi_made")
                self.w_lo = slots(f"{n}_w_lo_made")
                self.used = slots(f"{n}_used")
                self.listed = sem(f"{n}_listed")
                self.relisted = sem(f"{n}_relisted")
                self.gathered = sem(f"{n}_gathered")
                self.x_turned = slots(f"{n}_x_turned")
                self.x_in = slots(f"{n}_x_in")
                self.x_hi = slots(f"{n}_x_hi")
                self.x_lo = slots(f"{n}_x_lo")
                self.silued = slots(f"{n}_silued")
                self.hidden = slots(f"{n}_hidden")
                self.h_turned = slots(f"{n}_h_turned")
                self.h_hi = slots(f"{n}_h_hi")
                self.h_lo = slots(f"{n}_h_lo")
                self.y_out = slots(f"{n}_y_out")
                self.scattered = sem(f"{n}_scattered")

            def number(self, run, e, i):
                return 12 * e + i - (0 if run == "first" else 4)

            def raw_slot(self, run, i):
                return (i + (0 if run == "first" else 8)) % RAW

            def part_slot(self, run, i):
                return (i + (0 if run == "first" else 2)) % PARTS

            def load(self, sp, run, e, i, first=False):
                m, s = i // NS, i % NS
                src = (w_gate, w_up, w_down)[m].rearrange("l e k n -> (l e) k n")[e - (m == 2)]
                if not first:
                    sp.wait_ge(self.w_lo, after(self.number(run, e, i) - RAW))
                slot = self.raw_slot(run, i)
                sp.dma_start(self.raw[:, slot], src[s * SL * P:(s + 1) * SL * P, :].rearrange("(c p) n -> p c n", p=P)
                             ).then_inc(self.w_in[slot], 16)

            def sp_first(self, l):
                def f(sp):
                    for i in range(2 * NS):
                        self.load(sp, "first", NE * l, i, first=(l == 0))
                    for i in range(NS):
                        self.load(sp, "step", NE * l + 1, i, first=(l == 0))
                return f

            def sp(self, l):
                def f(sp):
                    e0, e1 = NE * l, NE * l + NE
                    for i in range(NS + PARTS, 3 * NS):
                        self.load(sp, "step", e0 + 1, i)
                    with sp.Fori(e0 + 2, e1) as e:
                        for i in range(3 * NS):
                            self.load(sp, "step", e, i)
                    for s in range(NS):
                        slot = self.raw_slot("step", s)
                        sp.wait_ge(self.w_lo, after(self.number("step", e1, s) - RAW))
                        sp.dma_start(self.raw[:, slot], w_down[l, NE - 1, s * SL * P:(s + 1) * SL * P, :].rearrange("(c p) n -> p c n", p=P)
                                     ).then_inc(self.w_in[slot], 16)
                return f

            def sp_early(self, l):
                def f(sp):
                    for i in range(NS, NS + PARTS):
                        self.load(sp, "step", NE * l + 1, i)
                return f

            def act_split_early(self, l):
                return lambda act: [self.split_hi(act, "first", NE * l, i) for i in range(PARTS)]

            def pool_split_early(self, l):
                return lambda pool: [self.split_lo(pool, "first", NE * l, i) for i in range(PARTS)]

            def split_hi(self, act, run, e, i):
                n, slot = self.number(run, e, i), self.raw_slot(run, i)
                uses = e + 1 - (run != "first" and i < 4)
                act.wait_ge(self.w_in[slot], 16 * uses)
                act.wait_ge(self.used, after(n - PARTS))
                act.activation(w_hi[:, self.part_slot(run, i)], self.raw[:, slot], ACT.Copy).then_inc(self.w_hi, 1)

            def split_lo(self, dve, run, e, i):
                n, slot = self.number(run, e, i), self.part_slot(run, i)
                dve.wait_ge(self.w_hi, after(n))
                dve.tensor_tensor(w_lo[:, slot], self.raw[:, self.raw_slot(run, i)], w_hi[:, slot].bitcast(F32),
                                  ALU.subtract).then_inc(self.w_lo, 1)

            def product(self, pe, run, e, i0, bank, a_hi, a_lo):
                for i in range(i0, i0 + NS):
                    pe.wait_ge(self.w_lo, after(self.number(run, e, i)))
                    slot = self.part_slot(run, i)
                    for j in range(SL):
                        c = (i - i0) * SL + j
                        passes = [(a_hi, w_hi), (a_lo, w_hi), (a_hi, w_lo)]
                        for n, (a, w) in enumerate(passes):
                            for half in range(2):
                                last = pe.matmul(bank[:CAP, half], a[:, c], w[:, slot, j, half * 512:(half + 1) * 512],
                                                 start=(c == 0 and n == 0), stop=(c == DC - 1 and n == 2))
                    last.then_inc(self.used, 1)

            def pe_turn_x(self, pe, e):
                pe.wait_ge(self.gathered, 16 * e + 16)
                pe.wait_ge(self.h_lo, after(e - 2))
                settle(pe)
                for c in range(DC):
                    last = pe.transpose(o_ps[:, c // 4, (c % 4) * CAP:(c % 4 + 1) * CAP], self.xe[:CAP, c * P:(c + 1) * P], ident[:CAP, :CAP])
                last.then_inc(self.x_turned, 1)

            def pe_gate_up(self, pe, run, e):
                pe.wait_ge(self.x_lo, after(e))
                pe.wait_ge(self.silued, after(e - 1))
                self.product(pe, run, e, 0, proj_ps, x_hi, x_lo)
                pe.wait_ge(self.hidden, after(e - 1))
                self.product(pe, run, e, NS, score_ps, x_hi, x_lo)

            def pe_down(self, pe, run_e, e, i0):
                pe.wait_ge(self.h_lo, after(e))
                pe.wait_ge(self.y_out, after(e - 1))
                self.product(pe, "step", run_e, i0, pT_ps, h_hi, h_lo)

            def pe_turn_h(self, pe, e, last_one=False):
                pe.wait_ge(self.hidden, after(e))
                pe.wait_ge(self.x_in, after(e if last_one else e + 1))
                settle(pe)
                for c in range(DC):
                    last = pe.transpose(o_ps[:, c // 4, (c % 4) * CAP:(c % 4 + 1) * CAP], self.hid[:CAP, c * P:(c + 1) * P], ident[:CAP, :CAP])
                last.then_inc(self.h_turned, 1)

            def pe(self, l):
                def f(pe):
                    e0, e1 = NE * l, NE * l + NE
                    self.pe_turn_x(pe, e0)
                    self.pe_gate_up(pe, "first", e0)
                    self.pe_turn_x(pe, e0 + 1)
                    self.pe_turn_h(pe, e0)
                    with pe.Fori(e0 + 1, e1 - 1) as e:
                        self.pe_gate_up(pe, "step", e)
                        self.pe_turn_x(pe, e + 1)
                        self.pe_down(pe, e, e - 1, 2 * NS)
                        self.pe_turn_h(pe, e)
                    self.pe_gate_up(pe, "step", e1 - 1)
                    self.pe_down(pe, e1 - 1, e1 - 2, 2 * NS)
                    self.pe_turn_h(pe, e1 - 1, last_one=True)
                    self.pe_down(pe, e1, e1 - 1, 0)
                return f

            def act_x(self, act, e):
                act.wait_ge(self.x_in, after(e))
                act.activation(x_hi[:], self.xeT, ACT.Copy).then_inc(self.x_hi, 1)

            def act_h(self, act, e):
                act.wait_ge(self.h_turned, after(e))
                act.activation(h_hi[:].rearrange("p (b c) t -> p b (c t)", b=2), o_ps[:, :, 0:4 * CAP], ACT.Copy).then_inc(self.h_hi, 1)

            def act_silu(self, act, run, e):
                act.wait_ge(self.used, after(self.number(run, e, NS - 1)))
                act.wait_ge(self.hidden, after(e - 1))
                act.activation(self.silu[:CAP, :], proj_ps[:CAP].rearrange("p b n -> p (b n)"), ACT.Silu).then_inc(self.silued, 1)

            def act_y(self, act, e, run_e, i_last, first=False):
                act.wait_ge(self.used, after(self.number("step", run_e, i_last)))
                if not first:
                    act.wait_ge(self.scattered, 16 * e)
                gate = gateT[:CAP, bass.ds(e, 1)]
                act.activation(self.y[:CAP, :], pT_ps[:CAP].rearrange("p b n -> p (b n)"), ACT.Copy, scale=gate).then_inc(self.y_out, 1)

            def act_step(self, act, e, y=True, first=False, x_next=True):
                for i in range(3 * NS):
                    self.split_hi(act, "step", e, i)
                    if i == 2:
                        if y:
                            self.act_y(act, e - 2, e - 1, 3 * NS - 1, first)
                        self.act_h(act, e - 1)
                    if i == NS + 2:
                        self.act_silu(act, "step", e)
                if x_next:
                    self.act_x(act, e + 1)

            def act(self, l):
                def f(act):
                    e0, e1 = NE * l, NE * l + NE
                    self.act_x(act, e0)
                    for i in range(PARTS, 2 * NS):
                        self.split_hi(act, "first", e0, i)
                        if i == NS + 2:
                            self.act_silu(act, "first", e0)
                    self.act_x(act, e0 + 1)
                    self.act_step(act, e0 + 1, y=False)
                    self.act_step(act, e0 + 2, first=(l == 0))
                    with act.Fori(e0 + 3, e1 - 1) as e:
                        self.act_step(act, e)
                    self.act_step(act, e1 - 1, x_next=False)
                    for i in range(NS):
                        self.split_hi(act, "step", e1, i)
                        if i == 2:
                            self.act_y(act, e1 - 2, e1 - 1, 3 * NS - 1)
                            self.act_h(act, e1 - 1)
                    self.act_y(act, e1 - 1, e1, NS - 1)
                return f

            def dve_x(self, dve, l, e):
                dve.wait_ge(self.x_turned, after(e))
                g = g_of[f"ffn{l}"]
                for half in range(2):
                    last = dve.tensor_tensor(self.xeT[:, 4 * half:4 * half + 4], o_ps[:, half, 0:4 * CAP].rearrange("p (c t) -> p c t", c=4),
                                             g[:, 4 * half:4 * half + 4].unsqueeze(2).to_broadcast([P, 4, CAP]), ALU.mult)
                last.then_inc(self.x_in, 1)

            def dve_x_lo(self, dve, e):
                dve.wait_ge(self.x_hi, after(e))
                dve.tensor_tensor(x_lo[:], self.xeT, x_hi[:].bitcast(F32), ALU.subtract).then_inc(self.x_lo, 1)

            def dve_h_lo(self, dve, e):
                dve.wait_ge(self.h_hi, after(e))
                dve.tensor_tensor(h_lo[:].rearrange("p (b c) t -> p b (c t)", b=2), o_ps[:, :, 0:4 * CAP],
                                  h_hi[:].bitcast(F32).rearrange("p (b c) t -> p b (c t)", b=2), ALU.subtract).then_inc(self.h_lo, 1)

            def dve_hid(self, dve, run, e):
                dve.wait_ge(self.silued, after(e))
                dve.wait_ge(self.used, after(self.number(run, e, 2 * NS - 1)))
                dve.wait_ge(self.h_turned, after(e - 1))
                dve.tensor_tensor(self.hid[:CAP, :], self.silu[:CAP, :], score_ps[:CAP].rearrange("p b n -> p (b n)"),
                                  ALU.mult).then_inc(self.hidden, 1)

            def dve_step(self, dve, l, e, x_next=True):
                for i in range(3 * NS):
                    self.split_lo(dve, "step", e, i)
                    if i == 3:
                        self.dve_h_lo(dve, e - 1)
                    if i == 2 * NS + 2:
                        if x_next:
                            self.dve_x(dve, l, e + 1)
                        self.dve_hid(dve, "step", e)
                if x_next:
                    self.dve_x_lo(dve, e + 1)

            def dve(self, l):
                def f(dve):
                    e0, e1 = NE * l, NE * l + NE
                    self.dve_x(dve, l, e0)
                    self.dve_x_lo(dve, e0)
                    for i in range(PARTS, 2 * NS):
                        self.split_lo(dve, "first", e0, i)
                    self.dve_x(dve, l, e0 + 1)
                    self.dve_hid(dve, "first", e0)
                    self.dve_x_lo(dve, e0 + 1)
                    with dve.Fori(e0 + 1, e1 - 1) as e:
                        self.dve_step(dve, l, e)
                    self.dve_step(dve, l, e1 - 1, x_next=False)
                    for i in range(NS):
                        self.split_lo(dve, "step", e1, i)
                        if i == 2:
                            self.dve_h_lo(dve, e1 - 1)
                return f

            def gather(self, pool, l, e, first=False):
                if not first:
                    pool.wait_ge(self.gathered, 16 * e)
                pool.wait_ge(self.x_turned, after(e - 1))
                pool.tensor_copy(self.gather_idx[:CAP, :], idxT[:CAP, bass.ds(e, 1)]).then_inc(self.listed, 1)
                pool.wait_ge(self.listed, e + 1)
                settle(pool)
                pool.indirect_dma_start(self.xe[:CAP, :], None, xn_dram[l],
                                        bass.IndirectOffsetOnAxis(self.gather_idx[:CAP, :], 0)).then_inc(self.gathered, 16)

            def scatter(self, pool, l, e):
                pool.wait_ge(self.y_out, after(e))
                pool.tensor_copy(self.scatter_idx[:CAP, :], idxT[:CAP, bass.ds(e, 1)]).then_inc(self.relisted, 1)
                pool.wait_ge(self.relisted, e + 1)
                settle(pool)
                pool.indirect_dma_start(acc_dram[l], bass.IndirectOffsetOnAxis(self.scatter_idx[:CAP, :], 0),
                                        self.y[:CAP, :], None, compute_op=ALU.add).then_inc(self.scattered, 16)

            def pool(self, l):
                def f(pool):
                    e0, e1 = NE * l, NE * l + NE
                    self.gather(pool, l, e0, l == 0)
                    self.gather(pool, l, e0 + 1)
                    with pool.Fori(e0 + 1, e1 - 1) as e:
                        self.gather(pool, l, e + 1)
                        self.scatter(pool, l, e - 1)
                    self.scatter(pool, l, e1 - 2)
                    self.scatter(pool, l, e1 - 1)
                    pool.wait_ge(self.scattered, 16 * e1)
                return f

        CONSTS = 48
        norms = {n: Norm(n, k) for k, n in enumerate(("mix0", "ffn0", "mix1", "ffn1", "final"))}
        mix_a, mix_b, mix_c = MixerA(), MixerB(), MixerC()
        outs = [OutProject(l) for l in range(2)]
        routes = [Route(l) for l in range(2)]
        experts = Experts()
        final = norms["final"]
        fc = Carve(8 * D)
        final_gain = fc(D)
        y_sb = fc(NT, D)
        final_in, final_y, final_stored = sem("final_gain_in"), sem("final_y"), sem("final_stored")

        def run(eng, steps):
            for n in phases:
                for f in steps.get(n, ()):
                    f(eng)
                if n != "final":
                    end_phase(eng, n)

        block = es.enter_context(nc.Block())

        @block.sync
        def _(sp):
            for s in seeded:
                sp.sem_inc(s, 2)

            def load_tiles(sp, src):
                for i in range(NT // 2):
                    sp.dma_start(x[:, 2 * i:2 * i + 2], src[2 * i * P:2 * (i + 1) * P].rearrange("(t p) n -> p t n", p=P)
                                 ).then_inc(x_loaded[i], 16)

            def load_x(sp):
                load_tiles(sp, x_in)
                sp.dma_start(ident[:], ident_in).then_inc(consts_in, 16)
                sp.dma_start(gcol[:], gains).then_inc(consts_in, 16)
                sp.dma_start(router_sb[:], router).then_inc(consts_in, 16)
                mix_a.sp_early(sp)
                mix_c.windows(sp)

            def reload_x(l, name):
                def f(sp):
                    load_tiles(sp, acc_dram[l])
                return f

            def store_rows(l):
                def f(sp):
                    nm = norms[f"ffn{l}"]
                    for t in range(NT):
                        sp.wait_ge(norm_scaled, nm.t0 + t + 1)
                        sp.dma_start(xn_dram[l][t * P:(t + 1) * P], nm.xn[:, t]).then_inc(rows_stored, 16)
                    experts.sp_first(l)(sp)
                    sp.wait_ge(rows_stored, 16 * 2 * NT * (l + 1))
                return f

            def store_x(l):
                def f(sp):
                    for t in range(NT):
                        sp.wait_ge(out_added, after(2 * NT * l + NT + t))
                        sp.dma_start(acc_dram[l][t * P:(t + 1) * P], x[:, t]).then_inc(rows_stored, 16)
                return f

            def a_stores_landed(sp):
                mix_a.stored(sp, sum(mix_a.tiles(g) for g in range(GROUPS)))

            def store_y(sp):
                for t in range(NT):
                    sp.wait_ge(final_y, t + 1)
                    sp.dma_start(y_out[t * P:(t + 1) * P], y_sb[:, t]).then_inc(final_stored, 16)
                sp.wait_ge(final_stored, 16 * NT)

            run(sp, {"mix0": [load_x], "a": [mix_a.sp, a_stores_landed], "join": [mix_a.join_sp, mix_b.sp_early], "b": [outs[0].sp, mix_b.sp], 
                     "out0": [store_x(0)], "ffn0": [store_rows(0)], "route0": [experts.sp_early(0)], "moe0": [experts.sp(0)],
                     "mix1": [reload_x(0, "mix1"), mix_c.sp_first, mix_c.sp_early], "c": [outs[1].sp, mix_c.sp],
                     "out1": [store_x(1)], "ffn1": [store_rows(1)], "route1": [experts.sp_early(1)], "moe1": [experts.sp(1)],
                     "final": [reload_x(1, "final"),
                               lambda sp: sp.dma_start(final_gain, final_g.to_broadcast([P, D])).then_inc(final_in, 16),
                               store_y]})

        @block.tensor
        def _(pe):
            run(pe, {"mix0": [norms["mix0"].pe], "a": [mix_a.pe], "join": [mix_b.latent_pe, mix_a.join_pe], "b": [mix_b.pe], "out0": [outs[0].pe],
                     "ffn0": [lambda pe: norms["ffn0"].pe(pe, routes[0].pe_logits)], "route0": [routes[0].pe], "moe0": [experts.pe(0)],
                     "mix1": [norms["mix1"].pe], "c": [mix_c.pe], "out1": [outs[1].pe],
                     "ffn1": [lambda pe: norms["ffn1"].pe(pe, routes[1].pe_logits)], "route1": [routes[1].pe], "moe1": [experts.pe(1)]})

        @block.scalar
        def _(act):
            run(act, {"mix0": [norms["mix0"].act], "a": [mix_a.act], "join": [mix_a.join_act, mix_b.latent_act], "b": [mix_b.act],
                      "out0": [outs[0].act, norms["ffn0"].act_squares], "ffn0": [norms["ffn0"].act], "route0": [routes[0].act, experts.act_split_early(0)], "moe0": [experts.act(0)],
                      "mix1": [norms["mix1"].act, lambda act: norms["mix1"].act_hi(act, {1: mix_c.act_early_v, 4: mix_c.act_early_qk})], "c": [mix_c.act],
                      "out1": [outs[1].act, norms["ffn1"].act_squares], "ffn1": [norms["ffn1"].act], "route1": [routes[1].act, experts.act_split_early(1)], "moe1": [experts.act(1)],
                      "final": [final.act]})

        @block.vector
        def _(dve):
            def final_dve(dve):
                final.dve_stats(dve)
                dve.wait_ge(final_in, 16)
                for t in range(NT):
                    dve.wait_ge(norm_scaled, final.t0 + t + 1)
                    dve.tensor_tensor(y_sb[:, t], final.xn[:, t], final_gain, ALU.mult).then_inc(final_y, 1)

            run(dve, {"mix0": [mix_a.dve_early, norms["mix0"].dve], "a": [mix_a.dve], "join": [lambda dve: mix_a.join_dve(dve, mix_b.latent_dve)], "b": [mix_b.dve], "out0": [outs[0].dve],
                      "ffn0": [norms["ffn0"].dve], "route0": [routes[0].dve], "moe0": [experts.dve(0)],
                      "mix1": [mix_c.dve_early, norms["mix1"].dve], "c": [mix_c.dve], "out1": [outs[1].dve],
                      "ffn1": [norms["ffn1"].dve], "route1": [routes[1].dve], "moe1": [experts.dve(1)],
                      "final": [final_dve]})

        @block.gpsimd
        def _(pool):
            run(pool, {"route0": [experts.pool_split_early(0)], "route1": [experts.pool_split_early(1)], "moe0": [experts.pool(0)], "mix1": [mix_c.pool_early], "c": [mix_c.pool], "moe1": [experts.pool(1)]})


def shape_constants():
    import numpy as np

    def bucket(rel):
        n = np.abs(rel)
        large = 8 + (np.log(np.maximum(n, 1) / 8) / np.log(1024 / 8) * 8).astype(np.int32)
        return np.where(rel > 0, 16, 0) + np.where(n < 8, n, np.minimum(large, 15))

    onehot = np.zeros((33, 1024), np.float32)
    for at, n, zero, kind in ((0, 512, 255, 0), (512, 256, 127, 1), (768, 256, 127, 2)):
        d = np.arange(n) - zero
        if kind == 0:
            ok, rel = np.abs(d) <= 64, d
        elif kind == 1:
            ok, rel = np.abs(d) <= 64, 4 * d
        else:
            ok, rel = (d % 4 == 0) & (np.abs(d) <= 256), 4 * d
        b = bucket(rel)
        for i in range(n):
            onehot[b[i] if ok[i] else 32, at + i] = 1.0

    col_mask = np.zeros((128, 7, 16), np.float32)
    c, kc = np.arange(16)[:, None], np.arange(16)[None]
    for first, j, deltas in ((0, 0, (0, 1)), (2, 1, (-1, 0, 1)), (5, 3, (-1, 0))):
        qcol = 16 * j + c
        start = np.clip(qcol - 8, 0, 48)
        for n, d in enumerate(deltas):
            key = 16 * (j + d) + kc
            m = np.where((key >= start) & (key < start + 16), 0.0, MASKED).astype(np.float32)
            col_mask[:, first + n] = np.tile(m, (8, 1))

    inv = 1.0 / (10000.0 ** (np.arange(0, 32, 2, dtype=np.float32) / 32))
    pos = np.concatenate([np.arange(PROMPT), np.arange(SAMPLE)]).astype(np.float32)
    ang = pos[:, None] * inv[None].astype(np.float32)
    cos, sin = np.cos(ang).astype(np.float32), np.sin(ang).astype(np.float32)
    scale = np.float32(96 ** -0.5)
    q_table = np.ascontiguousarray(np.concatenate([np.ones((64, TOK), np.float32), cos.T, cos.T, -sin.T, sin.T]) * scale).astype(np.float32)
    rope = np.ascontiguousarray(np.stack([cos, sin], 1).reshape(NT, P, 2, 16).transpose(1, 0, 2, 3))
    return onehot, col_mask, q_table, rope


def kernel(x_prompt, x_sample, ln_mix_g, w_in_even, g_qa, w_qb, g_kva, w_kvb, t5_table, w_out_even,
           w_in_odd, rpb, w_out_odd, ln_ffn_g, router, w_gate, w_up, w_down, final_g):
    import numpy as np
    import concourse.bacc as bacc
    from concourse.bass_utils import run_bass_kernel_spmd

    a = np.asarray

    def rows(w):
        return a(w).reshape(-1, P, w.shape[-1]).transpose(1, 0, 2)

    def column(g):
        return a(g).reshape(-1, P).T

    onehot, col_mask, q_table, rope = shape_constants()
    wa = a(w_in_even)[0][:, :A_IN].reshape(D, 3, GROUPS, AH * HD)
    wb = a(w_in_even)[0][:, A_IN:]
    qb = a(w_qb)[0].reshape(QR, 2 * B_PAIRS, 96)
    qb = np.concatenate([qb, qb[:, :, 80:96], qb[:, :, 64:80]], axis=2).reshape(3, P, B_PAIRS, 256)
    kvb = a(w_kvb)[0].reshape(2, P, B_PAIRS, 2, 2, HD).transpose(2, 1, 0, 4, 3, 5).reshape(B_PAIRS, P, 2, 256)
    wc = a(w_in_odd)[0].reshape(DC, P, 3, C_PAIRS // 2, 2, P).transpose(3, 2, 4, 1, 0, 5)
    wc_v = wc[:, 2].transpose(0, 2, 3, 1, 4).reshape(C_PAIRS // 2, 1, P, DC, 2 * P)
    wc_qk = wc[:, 0:2].transpose(0, 2, 3, 4, 1, 5).reshape(C_PAIRS // 2, 2, P, DC, 2 * P)
    wc = np.concatenate([wc_v, wc_qk], axis=1).reshape(3 * C_PAIRS // 2, P, DC, 2 * P)
    rpb_wide = np.zeros((2 * C_PAIRS, DROWS, 64), a(rpb).dtype)
    rpb_wide[:, :, 16:47] = a(rpb)[0]
    arrays = {
        "x_in": np.concatenate([a(x_prompt).reshape(-1, D), a(x_sample).reshape(-1, D)]),
        "gains": np.concatenate([column(ln_mix_g[0]), column(ln_ffn_g[0]), column(ln_mix_g[1]), column(ln_ffn_g[1]),
                                 column(g_qa[0]), column(g_kva[0])], axis=1),
        "w_a": np.stack([rows(wa[:, :, g].reshape(D, 768)) for g in range(GROUPS)]),
        "w_b": rows(wb),
        "w_qb_pairs": qb.transpose(2, 1, 0, 3),
        "w_kvb_pairs": kvb,
        "w_out": np.stack([rows(a(w_out_even)[0]), rows(a(w_out_odd)[0])]),
        "w_c": wc,
        "t5": a(t5_table),
        "onehot": onehot,
        "rpb_wide": rpb_wide,
        "router_cols": np.stack([rows(a(router)[0]), rows(a(router)[1])], axis=1),
        "w_gate": a(w_gate), "w_up": a(w_up), "w_down": a(w_down),
        "final_row": a(final_g).reshape(1, D),
        "ident_in": np.eye(P, dtype=np.float32),
        "col_mask": col_mask, "q_table": q_table, "rope_in": rope,
    }
    arrays = {k: np.ascontiguousarray(v) for k, v in arrays.items()}
    nc = bacc.Bacc("TRN2", target_bir_lowering=False, num_devices=1)
    aps = [nc.dram_tensor(k, v.shape, mybir.dt.from_np(v.dtype), kind="ExternalInput").ap() for k, v in arrays.items()]
    y = nc.dram_tensor("y_out", (TOK, D), F32, kind="ExternalOutput").ap()
    program(nc, *aps, y)
    got = run_bass_kernel_spmd(nc, [arrays], core_ids=[0]).results[0]["y_out"]
    return got[:PROMPT].reshape(1, PROMPT, D), got[PROMPT:].reshape(1, SAMPLE, D)
```
